# Optimizing a Trainium2 kernel written in Bass

```python
import jax, jax.numpy as jnp
from jax import lax
import numpy as np

D_MODEL = 1024
BATCH = 1
SEQ = 1024
DEPTH = 1

ATTN_HEADS = 8
KV_HEADS = 2
HEAD_DIM = 64
ATTN_WIDTH = ATTN_HEADS * HEAD_DIM
KV_WIDTH = KV_HEADS * HEAD_DIM
CONV_CHANNELS = D_MODEL - ATTN_WIDTH
MIX_WIDTH = ATTN_WIDTH + CONV_CHANNELS
IN_WIDTH = ATTN_WIDTH + 2 * KV_WIDTH + 2 * CONV_CHANNELS
CONV_KERNEL = 31
WINDOW = 128
BLOCK = 128
ROPE_THETA = 10000.0
PEER_HEADS = 8
N_KEYS = 128
N_EXPERTS = N_KEYS * N_KEYS
PEER_QDIM = 256
PEER_TOPK = 16
PEER_BLOCK = 128
EPS = 1e-6
NEG = -1e30

kernel_name = "hymba_conformer_swa_peer_block"

def rms_norm(x, g):
    xf = x.astype(jnp.float32)
    y = xf * lax.rsqrt(jnp.mean(xf * xf, axis=-1, keepdims=True) + EPS)
    return (y * g.astype(jnp.float32)).astype(x.dtype)

def layer_norm(x, g, b):
    xf = x.astype(jnp.float32)
    mu = jnp.mean(xf, axis=-1, keepdims=True)
    xc = xf - mu
    y = xc * lax.rsqrt(jnp.mean(xc * xc, axis=-1, keepdims=True) + EPS)
    return (y * g.astype(jnp.float32) + b.astype(jnp.float32)).astype(x.dtype)

def rope(x, pos):
    half = x.shape[-1] // 2
    inv = ROPE_THETA ** (-jnp.arange(half, dtype=jnp.float32) / half)
    ang = pos.astype(jnp.float32)[:, None] * inv[None, :]
    cos = jnp.cos(ang)[None, :, None, :]
    sin = jnp.sin(ang)[None, :, None, :]
    xf = x.astype(jnp.float32)
    x1, x2 = xf[..., :half], xf[..., half:]
    return jnp.concatenate([x1 * cos - x2 * sin, x2 * cos + x1 * sin], axis=-1).astype(x.dtype)

def sliding_window_attention(q, k, v, sinks):
    B, S, H, d = q.shape
    nb = S // BLOCK
    G = H // KV_HEADS
    qb = q.reshape(B, nb, BLOCK, KV_HEADS, G, d)
    kb = k.reshape(B, nb, BLOCK, KV_HEADS, d)
    vb = v.reshape(B, nb, BLOCK, KV_HEADS, d)
    pad = ((0, 0), (1, 0), (0, 0), (0, 0), (0, 0))
    kcat = jnp.concatenate([jnp.pad(kb, pad)[:, :-1], kb], axis=2)
    vcat = jnp.concatenate([jnp.pad(vb, pad)[:, :-1], vb], axis=2)
    s = jnp.einsum('bnqhgd,bnkhd->bnhgqk', qb, kcat).astype(jnp.float32) * (d ** -0.5)
    qi = jnp.arange(BLOCK)[:, None]
    kj = jnp.arange(2 * BLOCK)[None, :]
    rel = qi + BLOCK - kj
    band = (rel >= 0) & (rel < WINDOW)
    exists = (jnp.arange(nb)[:, None, None] > 0) | (kj[None] >= BLOCK)
    mask = band[None] & exists
    s = jnp.where(mask[None, :, None, None], s, NEG)
    sink = sinks.astype(jnp.float32).reshape(KV_HEADS, G)[None, None, :, :, None, None]
    m = jnp.maximum(jnp.max(s, axis=-1, keepdims=True), sink)
    p = jnp.exp(s - m)
    p = p / (jnp.sum(p, axis=-1, keepdims=True) + jnp.exp(sink - m))
    o = jnp.einsum('bnhgqk,bnkhd->bnqhgd', p.astype(v.dtype), vcat)
    return o.reshape(B, S, H * d)

def conformer_conv(a, b, conv_w, conv_b, ln_g, ln_b):
    C = a.shape[-1]
    u = a * jax.nn.sigmoid(b)
    up = jnp.pad(u, ((0, 0), (CONV_KERNEL - 1, 0), (0, 0)))
    y = lax.conv_general_dilated(up, conv_w[:, None, :].astype(u.dtype), window_strides=(1,),
                                 padding='VALID', dimension_numbers=('NWC', 'WIO', 'NWC'),
                                 feature_group_count=C) + conv_b
    return jax.nn.silu(layer_norm(y, ln_g, ln_b))

def peer_ffn(x, w_q, sub_keys, u_tab, v_tab):
    B, S, D = x.shape
    xt = x.reshape(-1, PEER_BLOCK, D)

    def block(xb):
        T = xb.shape[0]
        q = (xb @ w_q).reshape(T, PEER_HEADS, 2, PEER_QDIM // 2)
        s = jnp.einsum('thpc,hpkc->thpk', q, sub_keys).astype(jnp.float32)
        top_s, top_i = lax.top_k(s, PEER_TOPK)
        cand = top_s[:, :, 0, :, None] + top_s[:, :, 1, None, :]
        best_s, best_c = lax.top_k(cand.reshape(T, PEER_HEADS, PEER_TOPK * PEER_TOPK), PEER_TOPK)
        i1 = jnp.take_along_axis(top_i[:, :, 0], best_c // PEER_TOPK, axis=-1)
        i2 = jnp.take_along_axis(top_i[:, :, 1], best_c % PEER_TOPK, axis=-1)
        ids = i1 * N_KEYS + i2
        g = jax.nn.softmax(best_s, axis=-1)
        ue = u_tab[ids]
        ve = v_tab[ids]
        act = jax.nn.gelu(jnp.einsum('td,thkd->thk', xb, ue).astype(jnp.float32), approximate=False)
        w = (g * act).astype(xb.dtype)
        return jnp.einsum('thk,thkd->td', w, ve)

    return lax.map(block, xt).reshape(B, S, D)

def setup_inputs(seed: int = 0) -> dict:
    key = jax.random.key(seed)
    ks = jax.random.split(key, 20)
    f32 = jnp.float32
    L = DEPTH

    def gain(k, n):
        return (1.0 + 0.02 * jax.random.normal(k, (L, n), f32))

    return {
        "x": jax.random.normal(ks[0], (BATCH, SEQ, D_MODEL), f32),
        "norm_mix_g": gain(ks[1], D_MODEL),
        "w_in": jax.random.normal(ks[2], (L, D_MODEL, IN_WIDTH), f32) * D_MODEL ** -0.5,
        "conv_w": jax.random.normal(ks[3], (L, CONV_KERNEL, CONV_CHANNELS), f32) * CONV_KERNEL ** -0.5,
        "conv_b": 0.02 * jax.random.normal(ks[4], (L, CONV_CHANNELS), f32),
        "conv_ln_g": gain(ks[5], CONV_CHANNELS),
        "conv_ln_b": 0.02 * jax.random.normal(ks[6], (L, CONV_CHANNELS), f32),
        "attn_sinks": 0.5 * jax.random.normal(ks[7], (L, ATTN_HEADS), f32),
        "attn_out_g": gain(ks[8], ATTN_WIDTH),
        "conv_out_g": gain(ks[9], CONV_CHANNELS),
        "w_out": jax.random.normal(ks[10], (L, MIX_WIDTH, D_MODEL), f32) * (0.5 * MIX_WIDTH ** -0.5),
        "norm_ffn_g": gain(ks[11], D_MODEL),
        "peer_w_q": jax.random.normal(ks[12], (L, D_MODEL, PEER_HEADS * PEER_QDIM), f32) * D_MODEL ** -0.5,
        "peer_sub_keys": jax.random.normal(ks[13], (L, PEER_HEADS, 2, N_KEYS, PEER_QDIM // 2), f32) * (PEER_QDIM // 2) ** -0.5,
        "peer_u": jax.random.normal(ks[14], (L, N_EXPERTS, D_MODEL), f32) * D_MODEL ** -0.5,
        "peer_v": jax.random.normal(ks[15], (L, N_EXPERTS, D_MODEL), f32) * 0.5,
        "final_norm_g": (1.0 + 0.02 * jax.random.normal(ks[16], (D_MODEL,), f32)),
    }

def reference(x, norm_mix_g, w_in, conv_w, conv_b, conv_ln_g, conv_ln_b, attn_sinks,
              attn_out_g, conv_out_g, w_out, norm_ffn_g, peer_w_q, peer_sub_keys,
              peer_u, peer_v, final_norm_g):
    B, S, _ = x.shape
    pos = jnp.arange(S, dtype=jnp.int32)
    splits = [ATTN_WIDTH, ATTN_WIDTH + KV_WIDTH, ATTN_WIDTH + 2 * KV_WIDTH,
              ATTN_WIDTH + 2 * KV_WIDTH + CONV_CHANNELS]
    h = x
    for l in range(DEPTH):
        hn = rms_norm(h, norm_mix_g[l])
        proj = hn @ w_in[l]
        q, k, v, ga, gb = jnp.split(proj, splits, axis=-1)
        q = rope(q.reshape(B, S, ATTN_HEADS, HEAD_DIM), pos)
        k = rope(k.reshape(B, S, KV_HEADS, HEAD_DIM), pos)
        v = v.reshape(B, S, KV_HEADS, HEAD_DIM)
        attn = sliding_window_attention(q, k, v, attn_sinks[l])
        conv = conformer_conv(ga, gb, conv_w[l], conv_b[l], conv_ln_g[l], conv_ln_b[l])
        mixed = jnp.concatenate([rms_norm(attn, attn_out_g[l]), rms_norm(conv, conv_out_g[l])], axis=-1)
        h = h + mixed @ w_out[l]
        hn = rms_norm(h, norm_ffn_g[l])
        h = h + peer_ffn(hn, peer_w_q[l], peer_sub_keys[l], peer_u[l], peer_v[l])
    return rms_norm(h, final_norm_g)


_drawn_inputs = setup_inputs


def setup_inputs(seed=0):
    import zlib

    import numpy as np

    out = dict(_drawn_inputs(seed))
    spreads = {}
    factors = {'conv_ln_b': 2.792,
     'attn_sinks': 8.0,
     'attn_out_g': 2.986,
     'conv_out_g': 2.864,
     'final_norm_g': 2.86}
    for name, (base, spread) in spreads.items():
        noise = np.random.default_rng([zlib.crc32(name.encode()), seed]).standard_normal(out[name].shape)
        drawn = base * np.exp(spread * noise) if base else spread * noise
        out[name] = __import__('jax').numpy.asarray(drawn.astype(out[name].dtype))
    for name, factor in factors.items():
        out[name] = (out[name] * factor).astype(out[name].dtype)
    return out
```

```python
from contextlib import ExitStack

import concourse.bass as bass
from concourse import mybir

P = 128
D = 1024
T = 1024
DK = D // P
NT = T // P
HEADS, KVH, HD = 8, 2, 64
GQ = HEADS // KVH
CONV = 512
CC = CONV // P
TAPS = 31
PH = 8
HP = 2 * PH
NKEY = 128
TOPK = 16
EPS = 1e-6
NEG = -1e30
LOWEST = -3.0e38
HALF = T // 2
HT = HALF // P
SUB = 64
HOT = 8
HQ = HOT // 4
SLOTS = 4
CREDIT = SLOTS * HQ
GC = 4
NG = NKEY // GC

CH_GATE, CH_K, CH_V, CH_Q = 0, 8, 9, 10
NCH = 14

C_ID, C_ONE, C_IOTA, C_ROT, C_MASK0, C_MASK, C_COS, C_SIN = 0, 128, 256, 384, 512, 768, 1024, 2048
C_END = 3072
G_MIX, G_FFN, G_ATT, G_CONV, B_CONV, LN_G, LN_B, SINK, CW = 0, 8, 16, 20, 24, 28, 32, 36, 44
G_EPS = CW + CC * TAPS
G_END = G_EPS + 1

F32 = mybir.dt.float32
F32R = mybir.dt.float32r
U32 = mybir.dt.uint32
ALU = mybir.AluOpType
ACT = mybir.ActivationFunctionType
AX = mybir.AxisListType


def decoder_block(nc, x, xT, w_in, w_out, w_q, keysT, uT, v_tab, consts, params, final_g, out, stop=99):
    gates = nc.dram_tensor("gates", (2, NKEY // 2, P, HALF // SUB, 2, SUB), F32, kind="Internal").ap()

    ctx = ExitStack()
    early = ExitStack()
    late = ExitStack()

    def sb(name, shape, dt=F32, where=ctx):
        return where.enter_context(nc.sbuf_tensor(name, shape, dt))

    def sem(name):
        return ctx.enter_context(nc.semaphore(name))

    with ctx:
        acc = sb("acc", [P, NT, D])
        hnT = sb("hnT", [P, DK, T])
        con = sb("con", [P, C_COS])
        par = sb("par", [P, G_END])
        small = sb("small", [P, 64])
        ident = con[:, C_ID:C_ID + P]
        ones = con[:, C_ONE:C_ONE + P]
        iota = con[:, C_IOTA:C_IOTA + P]

        rope = sb("rope", [P, 2, T], where=early)
        wide = sb("wide", [P, DK, T], where=early)
        wbuf = sb("wbuf", [P, 4, DK, P], where=early)
        ubuf = sb("ubuf", [P, CC, T + TAPS - 1], where=early)
        tmp = sb("tmp", [P, 2, T], where=early)
        tmp2 = sb("tmp2", [P, T], where=early)
        rb = sb("rb", [P, T], where=early)
        qT = sb("qT", [P, GQ, T], where=early)
        kT = sb("kT", [P, P + T], where=early)
        vv = sb("vv", [P, NT + 1, P], where=early)
        sm = sb("sm", [P, 3, GQ, 2 * P], where=early)
        pT = sb("pT", [P, 2 * GQ, P], where=early)
        att = sb("att", [P, 4, 6, GQ], where=early)
        tap = sb("tap", [P, 2, T], where=early)
        early.close()
        o_all = ubuf[:, :, :].rearrange("p c t -> p (c t)")[:, 0:NT * 512].rearrange("p (n d) -> p n d", n=NT)

        mid = ExitStack()
        s16 = sb("s16", [P, NT, HP, TOPK], where=mid)
        i16 = sb("i16", [P, NT, HP, TOPK], U32, where=mid)
        i16f = i16[:, :, :, :].bitcast(F32)
        scan = ExitStack()
        wqbuf = sb("wqbuf", [P, 4, DK, P], where=scan)
        qc = sb("qc", [P, 2, T], where=scan)
        keys = sb("keys", [P, HP, NKEY], where=scan)
        swork = sb("swork", [P, NT, NKEY], where=scan)
        scan.close()
        pick = ExitStack()
        cand = sb("cand", [P, PH, TOPK * TOPK], where=pick)
        cand2 = sb("cand2", [P, PH, TOPK * TOPK], where=pick)
        best = sb("best", [P, PH, TOPK], where=pick)
        bpos = sb("bpos", [P, PH * TOPK], U32, where=pick)
        bdig = sb("bdig", [P, 2, PH * TOPK], U32, where=pick)
        bdigf = sb("bdigf", [P, 2, PH * TOPK], where=pick)
        sel3 = sb("sel3", [P, 3, P], where=pick)
        selT = sb("selT", [P, 3, P], where=pick)
        hot = sb("hot", [P, SLOTS, 2, HOT, P], where=pick)
        den = sb("den", [P, 2, PH], where=pick)
        gbuf = sb("gbuf", [P, 2, NKEY, SUB], where=pick)
        pick.close()
        mid.close()

        xh = sb("xh", [P, DK, HALF], F32R, where=late)
        xl = sb("xl", [P, DK, HALF], F32R, where=late)
        u_raw = sb("u_raw", [P, 2, D], where=late)
        uh = sb("uh", [P, 2, DK, P], F32R, where=late)
        ul = sb("ul", [P, 2, DK, P], F32R, where=late)
        v_raw = sb("v_raw", [P, GC, D], where=late)
        vh = sb("vh", [P, GC, D], F32R, where=late)
        vl = sb("vl", [P, GC, D], F32R, where=late)
        gt = sb("gt", [P, GC // 2, HALF // SUB, 2, SUB], where=late)
        hg = sb("hg", [P, 2, HALF], where=late)
        wh = sb("wh", [P, GC, HALF], F32R, where=late)
        wl = sb("wl", [P, GC, HALF], F32R, where=late)
        late.close()
        fin = ExitStack()
        fg = sb("fg", [P, D], where=fin)
        fo = sb("fo", [P, 2, D], where=fin)
        fscr = sb("fscr", [P, D], where=fin)
        fin.close()

        ps = ctx.enter_context(nc.psum_tensor("ps", [P, 8, 512], F32))

        sq4 = [P, PH, TOPK, TOPK]
        c4 = cand[:, :, :].rearrange("p h (a b) -> p h a b", a=TOPK)
        c4b = cand2[:, :, :].rearrange("p h (a b) -> p h a b", a=TOPK)

        def bank2(b):
            return ps[:, b:b + 2, :].rearrange("p b n -> p (b n)")

        consts_in, rope_in, params_in = sem("consts_in"), sem("rope_in"), sem("params_in")
        xT_in = [sem(f"xT_in{k}") for k in range(DK)]
        x_in = sem("x_in")
        w_in_slot = [sem(f"w_in_slot{k}") for k in range(4)]
        wq_in_slot = [sem(f"wq_in_slot{k}") for k in range(4)]
        wout_in, keys_in = sem("wout_in"), sem("keys_in")
        def sems(names):
            return [sem(n) for n in names.split()]

        pads_ready, sq_ready, sq_used, rms_root, hn_ready = sems("pads_ready sq_ready sq_used rms_root hn_ready")
        proj_ready = sem("proj_ready")
        pair_free = [sem("pair_free0"), sem("pair_free1")]
        raw_ready, rot_ready, rope_done, v_copied = sems("raw_ready rot_ready rope_done v_copied")
        gate_out, conv_dve, conv_pool = sems("gate_out conv_dve conv_pool")
        ln_sum, ln_stat, ln_y, ln_sq, ln_used = sems("ln_sum ln_stat ln_y ln_sq ln_used")
        sc_ready, sm_ready, sc_free, p_ready, pt_ready, pt_copied, o_ready, o_done = sems(
            "sc_ready sm_ready sc_free p_ready pt_ready pt_copied o_ready o_done")
        ao_root, ao_rec, ao_scaled, ao_t, ao_mixed = sems("ao_root ao_rec ao_scaled ao_t ao_mixed")
        wo_ready, h_ready, h_root, h_rec, h_scaled, h_t, hnT_ready = sems(
            "wo_ready h_ready h_root h_rec h_scaled h_t hnT_ready")
        q_ready, q_copied, ks_ready, ks_free = sems("q_ready q_copied ks_ready ks_free")
        best_ready, exp_ready, dig_ready, idx_ready, sel_ready, selT_ps, selT_ready = sems(
            "best_ready exp_ready dig_ready idx_ready sel_ready selT_ps selT_ready")
        hot_eq, hot_ready, gp_ready, gp_free = sems("hot_eq hot_ready gp_ready gp_free")
        gates_out = [sem("gates_out0"), sem("gates_out1")]
        xh_ready, xl_ready = sem("xh_ready"), sem("xl_ready")
        u_in = [sem(f"u_in{k}") for k in range(2)]
        v_in = [sem(f"v_in{k}") for k in range(GC)]
        g_in = [sem(f"g_in{k}") for k in range(GC // 2)]
        uh_ready, ul_ready, vh_ready, vl_ready = sems("uh_ready ul_ready vh_ready vl_ready")
        hp_ready, gelu_ready, w_ready, wh_ready, wl_ready = sems("hp_ready gelu_ready w_ready wh_ready wl_ready")
        op_ready, op_free = sems("op_ready op_free")
        f_root, f_ready, fg_in = sems("f_root f_ready fg_in")
        f_out = [sem("f_out0"), sem("f_out1")]

        block = ctx.enter_context(nc.Block())
        STEPS = [(n, g) for n in range(NT) for g in range(KVH)]
        NS = len(STEPS)
        PAIR = [0, 2] * (NCH // 2)
        TOKENS_HOT = 8
        ROPED = 1 + GQ

        @block.sync
        def _(sp):
            sp.dma_start(con[:, :], consts[:, 0:C_COS]).then_inc(consts_in, 16)
            sp.dma_start(par[:, :], params).then_inc(params_in, 16)
            for k in range(DK):
                sp.dma_start(wide[:, k, :], xT[:, k, :]).then_inc(xT_in[k], 16)
            for c in range(4):
                sp.dma_start(wbuf[:, c, :, :], w_in[c]).then_inc(w_in_slot[c], 16)
            sp.dma_start(rope[:, :, :], consts[:, C_COS:C_END].rearrange("p (s t) -> p s t", s=2)).then_inc(rope_in, 16)
            for c in range(4, NCH):
                sp.wait_ge(proj_ready, c - 3)
                sp.dma_start(wbuf[:, c % 4, :, :], w_in[c]).then_inc(w_in_slot[c % 4], 16)
            sp.dma_start(acc[:, :, :], x.rearrange("(n p) d -> p n d", p=P)).then_inc(x_in, 16)
            sp.wait_ge(proj_ready, NCH)
            sp.dma_start(wide[:, :, :], w_out).then_inc(wout_in, 16)
            sp.wait_ge(wo_ready, NT)
            sp.wait_ge(hnT_ready, NT)
            sp.dma_start(keys[:, :, :], keysT).then_inc(keys_in, 16)
            for c in range(HP):
                if c >= 4:
                    sp.wait_ge(q_ready, c - 3)
                sp.dma_start(wqbuf[:, c % 4, :, :], w_q[c]).then_inc(wq_in_slot[c % 4], 16)
            for half in range(2):
                with sp.Fori(0, HT) as i:
                    for b in range(2):
                        sp.wait_ge(gp_free, (half * NT + i * 2 + b + 1) * (SUB // 4) + 2)
                        sp.dma_start(gates[half, :, :, i * 2 + b, :, :].rearrange("j p e c -> p j (e c)"),
                                     gbuf[:, b, :, :].rearrange("p (j e) c -> p j (e c)", e=2)).then_inc(gates_out[b], 16)
            for b in range(2):
                sp.wait_ge(gates_out[b], 16 * NT)

            def load_group(half, g, first=False):
                for c in range(GC):
                    n = half * NKEY + g * GC + c
                    if not first or c >= 2:
                        sp.wait_ge(uh_ready, n - 1)
                        sp.wait_ge(ul_ready, n - 1)
                    sp.dma_start(u_raw[:, c % 2, :], uT[g * GC + c]).then_inc(u_in[c % 2], 16)
                    if not first:
                        sp.wait_ge(vh_ready, n - GC + 1)
                        sp.wait_ge(vl_ready, n - GC + 1)
                    sp.dma_start(v_raw[:, c, :], v_tab[g * GC + c]).then_inc(v_in[c], 16)
                    if c % 2 == 0:
                        if not first:
                            sp.wait_ge(w_ready, n - 2)
                        sp.dma_start(gt[:, c // 2, :, :, :], gates[half, g * (GC // 2) + c // 2]).then_inc(g_in[c // 2], 16)

            load_group(0, 0, first=True)
            with sp.Fori(1, NG) as g:
                load_group(0, g)
            with sp.Fori(0, NG) as g:
                load_group(1, g)
            sp.wait_ge(op_free, 2 * NG * 8)
            sp.dma_start(fg[:, :], final_g.partition_broadcast(P)).then_inc(fg_in, 16)
            for n in range(NT):
                sp.wait_ge(f_ready, n + 1)
                sp.dma_start(out[n * P:(n + 1) * P, :], fo[:, n % 2, :]).then_inc(f_out[n % 2], 16)
            for b in range(2):
                sp.wait_ge(f_out[b], 16 * (NT // 2))

        @block.gpsimd
        def _(pool):
            nc.gpsimd.memset(ubuf[:, :, 0:TAPS - 1], 0.0)
            nc.gpsimd.memset(kT[:, 0:P], 0.0)
            nc.gpsimd.memset(vv[:, 0, :], 0.0).then_inc(pads_ready, 1)
            pool.wait_ge(pads_ready, 1)
            for c in (0, CC - 1):
                u, y = ubuf[:, c, TAPS - 1:], hnT[:, 4 + c, :]
                pool.wait_ge(gate_out, 2 * c + 2)
                nc.gpsimd.tensor_tensor(u, u, y, ALU.mult)
                pool.drain()
                nc.gpsimd.tensor_scalar(y, ubuf[:, c, 0:T], par[:, CW + c * TAPS:CW + c * TAPS + 1],
                                        par[:, B_CONV + c:B_CONV + c + 1], ALU.mult, ALU.add)
                for k in range(1, TAPS):
                    nc.gpsimd.tensor_scalar(tap[:, k % 2, :], ubuf[:, c, k:k + T],
                                            par[:, CW + c * TAPS + k:CW + c * TAPS + k + 1], 0.0, ALU.mult, ALU.add)
                    pool.drain()
                    nc.gpsimd.tensor_tensor(y, y, tap[:, k % 2, :], ALU.add)
                pool.drain()
                pool.sem_inc(conv_pool, 1)

            with pool.Fori(0, NT) as i:
                it = i16f[:, bass.ds(i, 1), :, :].rearrange("p o (h s) k -> p (o h) s k", s=2)
                for d, cc in ((0, c4), (1, c4b)):
                    pool.wait_ge(dig_ready, i * 2 + d + 1)
                    nc.gpsimd.tensor_tensor(cc, cc, it[:, :, d, :].unsqueeze(2).to_broadcast(sq4),
                                            ALU.mult).then_inc(idx_ready, 1)
                with pool.Fori(0, P // (SLOTS * HOT)) as k:
                    for b in range(SLOTS):
                        pool.wait_ge(hot_eq, i * (P // HOT) + k * SLOTS + b + 1)
                        row = hot[:, b, 1, :, :]
                        nc.gpsimd.tensor_tensor(row, row, selT[:, 2, bass.ds((k * SLOTS + b) * HOT, HOT)].unsqueeze(2)
                                                .to_broadcast([P, HOT, P]), ALU.mult).then_inc(hot_ready, 1)

        @block.scalar
        def _(act):
            for k in range(DK):
                act.wait_ge(xT_in[k], 16)
                if k >= 2:
                    act.wait_ge(sq_used, k - 1)
                nc.scalar.activation(tmp[:, k % 2, :], wide[:, k, :], ACT.Square).then_inc(sq_ready, 1)
            act.wait_ge(sq_used, DK)
            act.wait_ge(params_in, 16)
            nc.scalar.activation(rb[:, :], bank2(0), ACT.Sqrt, bias=par[:, G_EPS:G_END], scale=1.0 / D).then_inc(rms_root, 1)

            def copy_raw(r, blk):
                act.wait_ge(proj_ready, blk + 1)
                if r >= 2:
                    act.wait_ge(rope_done, r - 1)
                nc.scalar.copy(tmp[:, r % 2, :], bank2(2 * (blk % 2))).then_inc(raw_ready, 1)

            for c in range(CC):
                act.wait_ge(proj_ready, CH_GATE + 2 * c + 1)
                nc.scalar.copy(ubuf[:, c, TAPS - 1:], bank2(0)).then_inc(gate_out, 1)
                act.wait_ge(proj_ready, CH_GATE + 2 * c + 2)
                nc.scalar.activation(hnT[:, 4 + c, :], bank2(2), ACT.Sigmoid).then_inc(gate_out, 1)
            copy_raw(0, CH_K)
            act.wait_ge(proj_ready, CH_V + 1)
            nc.scalar.copy(vv[:, 1:NT + 1, :].rearrange("p n d -> p (n d)"), bank2(2 * (CH_V % 2))).then_inc(v_copied, 1)
            for j in range(GQ):
                copy_raw(1 + j, CH_Q + j)

            def probs(s):
                act.wait_ge(sm_ready, s + 1)
                for j in range(GQ):
                    nc.scalar.activation(sm[:, s % 3, j, :], sm[:, s % 3, j, :], ACT.Exp, bias=att[:, s % 4, 1, j:j + 1],
                                         accum_out=att[:, s % 4, 3, j:j + 1])
                nc.scalar.activation(att[:, s % 4, 4, :], att[:, s % 4, 2, :], ACT.Exp).then_inc(p_ready, 1)

            for s in range(NS + 1):
                if s < NS:
                    probs(s)
                if s:
                    act.wait_ge(pt_ready, s)
                    if s >= 2:
                        act.wait_ge(o_ready, s - 1)
                    nc.scalar.copy(pT[:, :, :].rearrange("p j q -> p (j q)"), bank2(4)).then_inc(pt_copied, 1)

            act.wait_ge(ln_sum, 1)
            nc.scalar.mul(rb[:, :], bank2(0), 1.0 / CONV).then_inc(ln_stat, 1)

            def squares(c, k, waits):
                act.wait_ge(ln_y, waits)
                if k >= 2:
                    act.wait_ge(ln_used, k - 1)
                nc.scalar.activation(tmp[:, k % 2, :], hnT[:, 4 + c, :], ACT.Square).then_inc(ln_sq, 1)

            for c in range(CC):
                squares(c, c, c + 1)
            act.wait_ge(ln_used, CC)
            nc.scalar.activation(rb[:, :], bank2(2), ACT.Sqrt, bias=par[:, G_EPS:G_END], scale=1.0 / CONV).then_inc(ln_stat, 1)
            for c in range(CC):
                act.wait_ge(ln_y, CC + c + 1)
                y = hnT[:, 4 + c, :]
                nc.scalar.activation(y, y, ACT.Silu, bias=par[:, LN_B + c:LN_B + c + 1], scale=par[:, LN_G + c:LN_G + c + 1])
                act.drain()
                if CC + c >= 2:
                    act.wait_ge(ln_used, CC + c - 1)
                nc.scalar.activation(tmp[:, c % 2, :], y, ACT.Square).then_inc(ln_sq, 1)
            act.wait_ge(ln_used, 2 * CC)
            nc.scalar.activation(rb[:, :], bank2(0), ACT.Sqrt, bias=par[:, G_EPS:G_END], scale=1.0 / CONV).then_inc(ln_stat, 1)

            for n in range(NT):
                act.wait_ge(o_done, 2 * n + 2)
                nc.scalar.activation(tmp2[:, 0:512], o_all[:, n, :], ACT.Square, accum_out=small[:, n:n + 1])
                act.drain()
            nc.scalar.activation(small[:, 8:16], small[:, 0:8], ACT.Sqrt, bias=par[:, G_EPS:G_END],
                                 scale=1.0 / 512).then_inc(ao_root, 1)
            act.wait_ge(ao_rec, 1)
            for n in range(NT):
                nc.scalar.mul(o_all[:, n, :], o_all[:, n, :], small[:, 16 + n:17 + n]).then_inc(ao_scaled, 1)

            def root(n):
                act.wait_ge(h_ready, n + 1)
                nc.scalar.activation(tmp2[:, :], acc[:, n, :], ACT.Square, accum_out=small[:, 24 + n:25 + n])
                act.drain()
                nc.scalar.activation(small[:, 32 + n:33 + n], small[:, 24 + n:25 + n], ACT.Sqrt,
                                     bias=par[:, G_EPS:G_END], scale=1.0 / D).then_inc(h_root, 1)

            for n in range(NT):
                root(n)
                act.wait_ge(h_rec, n + 1)
                if n >= 2:
                    act.wait_ge(h_t, n - 1)
                nc.scalar.mul(tmp[:, n % 2, :], acc[:, n, :], small[:, 40 + n:41 + n]).then_inc(h_scaled, 1)

            for c in range(HP):
                act.wait_ge(q_ready, c + 1)
                if c >= 2:
                    act.wait_ge(ks_ready, c - 1)
                nc.scalar.copy(qc[:, c % 2, :], bank2(2 * (c % 2))).then_inc(q_copied, 1)

            act.sem_inc(gp_free, 2)

            def gate_tile(i, first=False):
                act.wait_ge(best_ready, i + 1)
                nc.scalar.activation(best[:, :, :], best[:, :, :], ACT.Exp).then_inc(exp_ready, 1)
                act.wait_ge(selT_ps, i + 1)
                nc.scalar.copy(selT[:, :, :].rearrange("p k t -> p (k t)"), ps[:, 5, 0:3 * P]).then_inc(selT_ready, 1)
                for b in range(2):
                    if not first:
                        act.wait_ge(gates_out[b], 16 * i)
                    with act.Fori(0, SUB // 8) as k:
                        for e in range(2):
                            quad = i * (P // 4) + b * (SUB // 4) + k * 2 + e
                            act.wait_ge(gp_ready, CREDIT + quad + 1)
                            nc.scalar.copy(gbuf[:, b, :, bass.ds((k * 2 + e) * 4, 4)].rearrange("p i t -> p t i"),
                                           ps[:, 6 + e, :].rearrange("p (t i) -> p t i", t=4)).then_inc(gp_free, 1)

            gate_tile(0, first=True)
            with act.Fori(1, NT) as i:
                gate_tile(i)

            for b in range(2):
                act.wait_ge(gates_out[b], 16 * NT)

            def split_u(half, g, c):
                act.wait_ge(u_in[c % 2], 16 * (half * (NKEY // 2) + g * (GC // 2) + c // 2 + 1))
                nc.scalar.copy(uh[:, c % 2, :, :].rearrange("p k e -> p (k e)"), u_raw[:, c % 2, :]).then_inc(uh_ready, 1)

            def group(half, g, first=False, last=False):
                n0 = half * NKEY + g * GC
                if not first:
                    act.wait_ge(op_ready, (half * NG + g) * 8)
                for c in range(GC):
                    n = n0 + c
                    act.wait_ge(v_in[c], 16 * (half * NG + g + 1))
                    nc.scalar.copy(vh[:, c, :], v_raw[:, c, :]).then_inc(vh_ready, 1)
                    act.wait_ge(hp_ready, n + 1)
                    if not first or c >= 2:
                        act.wait_ge(wl_ready, n - 1)
                    nc.scalar.activation(hg[:, c % 2, :], ps[:, c % 2, :], ACT.Gelu).then_inc(gelu_ready, 1)
                    act.wait_ge(w_ready, n + 1)
                    nc.scalar.copy(wh[:, c, :], hg[:, c % 2, :]).then_inc(wh_ready, 1)
                    if c < 2:
                        split_u(half, g, c + 2)
                    elif not last:
                        split_u(half, g + 1, c - 2)

            for half in range(2):
                if half:
                    act.wait_ge(hp_ready, NKEY)
                for k in range(DK):
                    nc.scalar.copy(xh[:, k, :], hnT[:, k, half * HALF:(half + 1) * HALF]).then_inc(xh_ready, 1)
                split_u(half, 0, 0)
                split_u(half, 0, 1)
                if half == 0:
                    group(0, 0, first=True)
                with act.Fori(1 - half, NG - 1) as g:
                    group(half, g)
                group(half, NG - 1, last=True)

            act.wait_ge(op_free, 2 * NG * 8)
            for n in range(NT):
                nc.scalar.activation(fscr[:, :], acc[:, n, :], ACT.Square, accum_out=small[:, n:n + 1])
                act.drain()
            nc.scalar.activation(small[:, 8:16], small[:, 0:8], ACT.Sqrt, bias=par[:, G_EPS:G_END],
                                 scale=1.0 / D).then_inc(f_root, 1)

        @block.vector
        def _(dve):
            dve.wait_ge(rms_root, 1)
            nc.vector.reciprocal(rb[:, :], rb[:, :])
            dve.drain()
            for k in range(DK):
                nc.vector.scalar_tensor_tensor(out=wide[:, k, :], in0=wide[:, k, :], scalar=par[:, G_MIX + k:G_MIX + k + 1],
                                               in1=rb[:, :], op0=ALU.mult, op1=ALU.mult).then_inc(hn_ready, 1)

            dve.wait_ge(pads_ready, 1)
            for c in range(1, CC - 1):
                y = hnT[:, 4 + c, :]
                u = ubuf[:, c, TAPS - 1:]
                dve.wait_ge(gate_out, 2 * c + 2)
                nc.vector.tensor_tensor(u, u, y, ALU.mult)
                dve.drain()
                nc.vector.tensor_scalar(y, ubuf[:, c, 0:T], par[:, CW + c * TAPS:CW + c * TAPS + 1],
                                        par[:, B_CONV + c:B_CONV + c + 1], ALU.mult, ALU.add)
                dve.drain()
                with dve.Fori(0, (TAPS - 1) // 5) as r:
                    for j in range(5):
                        k = r * 5 + j + 1
                        nc.vector.scalar_tensor_tensor(out=y, in0=ubuf[:, c, bass.ds(k, T)],
                                                       scalar=par[:, bass.ds(k + CW + c * TAPS, 1)], in1=y,
                                                       op0=ALU.mult, op1=ALU.add)
                        dve.drain()
                dve.sem_inc(conv_dve, 1)

            dve.wait_ge(rope_in, 16)
            for r in range(1 + GQ):
                dst = kT[:, P:P + T] if r == 0 else qT[:, r - 1, :]
                dve.wait_ge(raw_ready, r + 1)
                nc.vector.tensor_tensor(dst, tmp[:, r % 2, :], rope[:, 0, :], ALU.mult)
                dve.wait_ge(rot_ready, r + 1)
                nc.vector.tensor_tensor(tmp2[:, :], bank2(4), rope[:, 1, :], ALU.mult)
                dve.drain()
                nc.vector.tensor_tensor(dst, dst, tmp2[:, :], ALU.add).then_inc(rope_done, 1)

            def soft(s):
                n, g = STEPS[s]
                b, m = s % 4, s % 3
                mask = con[:, C_MASK0:C_MASK0 + 2 * P] if n == 0 else con[:, C_MASK:C_MASK + 2 * P]
                sink = par[:, SINK + g * GQ:SINK + (g + 1) * GQ]
                dve.wait_ge(sc_ready, s + 1)
                if s >= 3:
                    dve.wait_ge(pt_ready, s - 2)
                nc.vector.scalar_tensor_tensor(
                    out=sm[:, m, :, :], in0=bank2(2 * (s % 2)).rearrange("p (j k) -> p j k", j=GQ), scalar=float(HD) ** -0.5,
                    in1=mask.unsqueeze(1).to_broadcast([P, GQ, 2 * P]), op0=ALU.mult, op1=ALU.add).then_inc(sc_free, 1)
                dve.drain()
                nc.vector.tensor_reduce(att[:, b, 0, :], sm[:, m, :, :], AX.X, ALU.max)
                dve.drain()
                nc.vector.tensor_tensor(att[:, b, 0, :], att[:, b, 0, :], sink, ALU.max)
                dve.drain()
                nc.vector.tensor_scalar(att[:, b, 1, :], att[:, b, 0, :], -1.0, None, ALU.mult)
                nc.vector.tensor_tensor(att[:, b, 2, :], sink, att[:, b, 0, :], ALU.subtract).then_inc(sm_ready, 1)

            def weighted(s):
                n, g = STEPS[s]
                b = s % 4
                dve.wait_ge(o_ready, s + 1)
                nc.vector.tensor_tensor(att[:, b, 3, :], att[:, b, 3, :], att[:, b, 4, :], ALU.add)
                dve.drain()
                nc.vector.reciprocal(att[:, b, 5, :], att[:, b, 3, :])
                dve.drain()
                if s == 0:
                    dve.wait_ge(conv_pool, 1)
                if s == 2 * 6:
                    dve.wait_ge(conv_pool, 2)
                nc.vector.tensor_tensor(
                    o_all[:, n, g * 256:(g + 1) * 256].rearrange("p (j d) -> p j d", j=GQ),
                    ps[:, 6 + s % 2, 0:256].rearrange("p (j d) -> p j d", j=GQ),
                    att[:, b, 5, :].unsqueeze(2).to_broadcast([P, GQ, HD]), ALU.mult).then_inc(o_done, 1)

            for s in range(NS + 2):
                if s < NS:
                    soft(s)
                if s >= 2:
                    weighted(s - 2)

            dve.wait_ge(ln_stat, 1)
            for c in range(CC):
                y = hnT[:, 4 + c, :]
                nc.vector.tensor_tensor(y, y, rb[:, :], ALU.subtract).then_inc(ln_y, 1)
            dve.wait_ge(ln_stat, 2)
            nc.vector.reciprocal(rb[:, :], rb[:, :])
            dve.drain()
            for c in range(CC):
                y = hnT[:, 4 + c, :]
                nc.vector.tensor_tensor(y, y, rb[:, :], ALU.mult).then_inc(ln_y, 1)
            dve.wait_ge(ln_stat, 3)
            nc.vector.reciprocal(rb[:, :], rb[:, :])
            dve.drain()
            for c in range(CC):
                y = hnT[:, 4 + c, :]
                nc.vector.scalar_tensor_tensor(out=y, in0=y, scalar=par[:, G_CONV + c:G_CONV + c + 1], in1=rb[:, :],
                                               op0=ALU.mult, op1=ALU.mult).then_inc(ln_y, 1)

            dve.wait_ge(ao_root, 1)
            nc.vector.reciprocal(small[:, 16:24], small[:, 8:16]).then_inc(ao_rec, 1)
            for n in range(NT):
                dve.wait_ge(ao_t, n + 1)
                nc.vector.tensor_tensor(
                    hnT[:, 0:4, n * P:(n + 1) * P], ps[:, 4 + n % 2, :].rearrange("p (m t) -> p m t", m=4),
                    par[:, G_ATT:G_ATT + 4].unsqueeze(2).to_broadcast([P, 4, P]), ALU.mult).then_inc(ao_mixed, 1)

            def normed(n):
                dve.wait_ge(h_t, n + 1)
                nc.vector.tensor_tensor(
                    hnT[:, :, n * P:(n + 1) * P], bank2(4 + 2 * (n % 2)).rearrange("p (m t) -> p m t", m=DK),
                    par[:, G_FFN:G_FFN + DK].unsqueeze(2).to_broadcast([P, DK, P]), ALU.mult).then_inc(hnT_ready, 1)

            dve.wait_ge(x_in, 16)
            for n in range(NT):
                dve.wait_ge(wo_ready, n + 1)
                nc.vector.tensor_tensor(acc[:, n, :], acc[:, n, :], bank2(2 * (n % 2)), ALU.add).then_inc(h_ready, 1)
                if n:
                    normed(n - 1)
                dve.wait_ge(h_root, n + 1)
                nc.vector.reciprocal(small[:, 40 + n:41 + n], small[:, 32 + n:33 + n]).then_inc(h_rec, 1)
            normed(NT - 1)

            for c in range(HP):
                dve.wait_ge(ks_ready, c + 1)
                sv = bank2(4 + 2 * (c % 2)).rearrange("p (n k) -> p n k", n=NT)
                for n in range(NT):
                    nc.vector.max(s16[:, n, c, 0:8], sv[:, n, :])
                dve.drain()
                for n in range(NT):
                    nc.vector.max_index(i16[:, n, c, 0:8], s16[:, n, c, 0:8], sv[:, n, :])
                for n in range(NT):
                    last = nc.vector.match_replace(swork[:, n, :], s16[:, n, c, 0:8], sv[:, n, :], LOWEST)
                last.then_inc(ks_free, 1)
                dve.drain()
                for n in range(NT):
                    nc.vector.max(s16[:, n, c, 8:16], swork[:, n, :])
                dve.drain()
                for n in range(NT):
                    nc.vector.max_index(i16[:, n, c, 8:16], s16[:, n, c, 8:16], swork[:, n, :])
            dve.drain()
            nc.vector.tensor_copy(i16f[:, :, :, :].rearrange("p n h k -> p (n h k)"),
                                  i16[:, :, :, :].rearrange("p n h k -> p (n h k)"))
            dve.drain()

            def pick_tile(i):
                st = s16[:, bass.ds(i, 1), :, :].rearrange("p o (h s) k -> p (o h) s k", s=2)
                nc.vector.tensor_tensor(c4, st[:, :, 0, :].unsqueeze(3).to_broadcast(sq4),
                                        st[:, :, 1, :].unsqueeze(2).to_broadcast(sq4), ALU.add)
                dve.drain()
                for h in range(PH):
                    nc.vector.max(best[:, h, 0:8], cand[:, h, :])
                dve.drain()
                for h in range(PH):
                    nc.vector.max_index(bpos[:, h * TOPK:h * TOPK + 8], best[:, h, 0:8], cand[:, h, :])
                for h in range(PH):
                    nc.vector.match_replace(cand2[:, h, :], best[:, h, 0:8], cand[:, h, :], LOWEST)
                dve.drain()
                for h in range(PH):
                    nc.vector.max(best[:, h, 8:16], cand2[:, h, :])
                dve.drain()
                for h in range(PH):
                    nc.vector.max_index(bpos[:, h * TOPK + 8:h * TOPK + 16], best[:, h, 8:16], cand2[:, h, :])
                nc.vector.tensor_copy(den[:, 0, :], best[:, :, 0])
                dve.drain()
                nc.vector.tensor_tensor(best[:, :, :], best[:, :, :], den[:, 0, :].unsqueeze(2).to_broadcast([P, PH, TOPK]),
                                        ALU.subtract).then_inc(best_ready, 1)
                nc.vector.tensor_scalar(bdig[:, 0, :], bpos[:, :], 4, None, ALU.logical_shift_right)
                nc.vector.tensor_scalar(bdig[:, 1, :], bpos[:, :], TOPK - 1, None, ALU.bitwise_and)
                dve.drain()
                nc.vector.tensor_copy(bdigf[:, :, :], bdig[:, :, :])
                dve.drain()
                for d, cc in ((0, c4), (1, c4b)):
                    dig = bdigf[:, d, :].rearrange("p (h k) -> p h k", h=PH)
                    nc.vector.tensor_tensor(cc, dig.unsqueeze(3).to_broadcast(sq4),
                                            iota[:, 0:TOPK].unsqueeze(1).unsqueeze(1).to_broadcast(sq4),
                                            ALU.is_equal).then_inc(dig_ready, 1)
                dve.wait_ge(exp_ready, i + 1)
                nc.vector.tensor_reduce(den[:, 1, :], best[:, :, :], AX.X, ALU.add)
                dve.drain()
                nc.vector.reciprocal(den[:, 0, :], den[:, 1, :])
                dve.drain()
                nc.vector.tensor_tensor(sel3[:, 2, :].rearrange("p (h k) -> p h k", h=PH), best[:, :, :],
                                        den[:, 0, :].unsqueeze(2).to_broadcast([P, PH, TOPK]), ALU.mult)

            def index_tile(i):
                for d, cc in ((0, c4), (1, c4b)):
                    dve.wait_ge(idx_ready, i * 2 + d + 1)
                    last = nc.vector.tensor_reduce(sel3[:, d, :].rearrange("p (h k) -> p h k", h=PH), cc, AX.X, ALU.add)
                last.then_inc(sel_ready, 1)

            def hot_tile(i):
                with dve.Fori(0, P // (SLOTS * HOT)) as k:
                    for b in range(SLOTS):
                        dve.wait_ge(selT_ready, i + 1)
                        dve.wait_ge(gp_ready, i * (P // 4) + (k * SLOTS + b + 1) * HQ)
                        nc.vector.tensor_tensor(
                            hot[:, b, :, :, :],
                            selT[:, 0:2, bass.ds((k * SLOTS + b) * HOT, HOT)].unsqueeze(3).to_broadcast([P, 2, HOT, P]),
                            iota.unsqueeze(1).unsqueeze(1).to_broadcast([P, 2, HOT, P]), ALU.is_equal).then_inc(hot_eq, 1)

            pick_tile(0)
            index_tile(0)
            with dve.Fori(0, NT - 1) as i:
                hot_tile(i)
                pick_tile(i + 1)
                index_tile(i + 1)
            hot_tile(NT - 1)

            def low_u(half, g, c):
                n = half * NKEY + g * GC + c
                dve.wait_ge(uh_ready, n + 1)
                nc.vector.tensor_tensor(ul[:, c % 2, :, :].rearrange("p k e -> p (k e)"), u_raw[:, c % 2, :],
                                        uh[:, c % 2, :, :].rearrange("p k e -> p (k e)").bitcast(F32),
                                        ALU.subtract).then_inc(ul_ready, 1)

            def group(half, g, first=False, last=False):
                n0 = half * NKEY + g * GC
                for c in range(GC):
                    n = n0 + c
                    dve.wait_ge(vh_ready, n + 1)
                    nc.vector.tensor_tensor(vl[:, c, :], v_raw[:, c, :], vh[:, c, :].bitcast(F32),
                                            ALU.subtract).then_inc(vl_ready, 1)
                    if c % 2 == 0:
                        dve.wait_ge(g_in[c // 2], 16 * (half * NG + g + 1))
                    dve.wait_ge(gelu_ready, n + 1)
                    nc.vector.tensor_tensor(hg[:, c % 2, :].rearrange("p (s t) -> p s t", t=SUB),
                                            hg[:, c % 2, :].rearrange("p (s t) -> p s t", t=SUB),
                                            gt[:, c // 2, :, c % 2, :], ALU.mult).then_inc(w_ready, 1)
                    dve.wait_ge(wh_ready, n + 1)
                    nc.vector.tensor_tensor(wl[:, c, :], hg[:, c % 2, :], wh[:, c, :].bitcast(F32),
                                            ALU.subtract).then_inc(wl_ready, 1)
                    if c < 2:
                        low_u(half, g, c + 2)
                    elif not last:
                        low_u(half, g + 1, c - 2)
                for k in range(8):
                    dve.wait_ge(op_ready, (half * NG + g) * 8 + k + 1)
                    dst = acc[:, half * HT + k % HT, (k // HT) * 512:(k // HT + 1) * 512]
                    nc.vector.tensor_tensor(dst, dst, ps[:, 2 + k % 4, :], ALU.add).then_inc(op_free, 1)

            for half in range(2):
                for k in range(DK):
                    dve.wait_ge(xh_ready, half * DK + k + 1)
                    nc.vector.tensor_tensor(xl[:, k, :], hnT[:, k, half * HALF:(half + 1) * HALF],
                                            xh[:, k, :].bitcast(F32), ALU.subtract).then_inc(xl_ready, 1)
                low_u(half, 0, 0)
                low_u(half, 0, 1)
                if half == 0:
                    group(0, 0, first=True)
                with dve.Fori(1 - half, NG - 1) as g:
                    group(half, g)
                group(half, NG - 1, last=True)

            dve.wait_ge(f_root, 1)
            nc.vector.reciprocal(small[:, 16:24], small[:, 8:16])
            dve.drain()
            dve.wait_ge(fg_in, 16)
            for n in range(NT):
                if n >= 2:
                    dve.wait_ge(f_out[n % 2], 16 * (n // 2))
                nc.vector.scalar_tensor_tensor(out=fo[:, n % 2, :], in0=acc[:, n, :], scalar=small[:, 16 + n:17 + n],
                                               in1=fg[:, :], op0=ALU.mult, op1=ALU.mult).then_inc(f_ready, 1)

        @block.tensor
        def _(pe):
            mm = nc.tensor.matmul
            pe.wait_ge(consts_in, 16)

            def sum_rows(bank, src, k, n):
                for hb in range(2):
                    last = mm(ps[:, bank + hb, :], ones, src[:, hb * 512:(hb + 1) * 512], start=k == 0, stop=k == n - 1)
                return last

            for k in range(DK):
                pe.wait_ge(sq_ready, k + 1)
                sum_rows(0, tmp[:, k % 2, :], k, DK).then_inc(sq_used, 1)

            def rotate(r):
                pe.wait_ge(raw_ready, r + 1)
                if r:
                    pe.wait_ge(rope_done, r)
                for hb in range(2):
                    last = mm(ps[:, 4 + hb, :], con[:, C_ROT:C_ROT + P], tmp[:, r % 2, hb * 512:(hb + 1) * 512],
                              start=True, stop=True)
                last.then_inc(rot_ready, 1)

            pe.wait_ge(rms_root, 1)
            for blk in range(NCH):
                pe.wait_ge(w_in_slot[blk % 4], 16 * (blk // 4 + 1))
                back = blk - 2
                if 0 <= back < CH_K:
                    pe.wait_ge(gate_out, back + 1)
                elif back == CH_K:
                    pe.wait_ge(raw_ready, 1)
                elif back == CH_V:
                    pe.wait_ge(v_copied, 1)
                elif back >= CH_Q:
                    pe.wait_ge(raw_ready, back - CH_Q + 2)
                w = wbuf[:, blk % 4, :, :]
                if blk == CH_V:
                    for n in range(NT):
                        for k in range(DK):
                            last = mm(ps[:, 2 + n // 4, (n % 4) * P:(n % 4 + 1) * P], wide[:, k, n * P:(n + 1) * P],
                                      w[:, k, :], start=k == 0, stop=k == DK - 1)
                else:
                    for k in range(DK):
                        if blk == 0:
                            pe.wait_ge(hn_ready, k + 1)
                        for hb in range(2):
                            last = mm(ps[:, 2 * (blk % 2) + hb, :], w[:, k, :], wide[:, k, hb * 512:(hb + 1) * 512],
                                      start=k == 0, stop=k == DK - 1)
                last.then_inc(proj_ready, 1)
                if blk == CH_V:
                    rotate(0)
                if blk > CH_Q:
                    rotate(blk - CH_Q)

            def scores(s):
                n, g = STEPS[s]
                if s >= 2:
                    pe.wait_ge(sc_free, s - 1)
                for j in range(GQ):
                    last = mm(ps[:, 2 * (s % 2) + j // 2, (j % 2) * 256:(j % 2 + 1) * 256],
                              qT[g * HD:(g + 1) * HD, j, n * P:(n + 1) * P], kT[g * HD:(g + 1) * HD, n * P:n * P + 2 * P],
                              start=True, stop=True)
                last.then_inc(sc_ready, 1)

            rotate(GQ)
            pe.wait_ge(rope_done, 1 + GQ)
            pe.wait_ge(pads_ready, 1)

            def turn_probs(s):
                pe.wait_ge(p_ready, s + 1)
                if s:
                    pe.wait_ge(pt_copied, s)
                for j in range(2 * GQ):
                    last = nc.tensor.transpose(ps[:, 4 + j // 4, (j % 4) * P:(j % 4 + 1) * P],
                                               sm[:, s % 3, j // 2, (j % 2) * P:(j % 2 + 1) * P], ident)
                last.then_inc(pt_ready, 1)

            def weigh(s):
                n, g = STEPS[s]
                pe.wait_ge(pt_copied, s + 1)
                if s >= 2:
                    pe.wait_ge(o_done, s - 1)
                for j in range(GQ):
                    for kb in range(2):
                        last = mm(ps[:, 6 + s % 2, j * HD:(j + 1) * HD], pT[:, 2 * j + kb, :],
                                  vv[:, n + kb, g * HD:(g + 1) * HD], start=kb == 0, stop=kb == 1)
                last.then_inc(o_ready, 1)

            scores(0)
            scores(1)
            for s in range(NS):
                turn_probs(s)
                if s + 2 < NS:
                    scores(s + 2)
                weigh(s)

            pe.wait_ge(sc_free, NS)
            pe.wait_ge(conv_dve, CC - 2)
            pe.wait_ge(conv_pool, 2)
            for c in range(CC):
                last = sum_rows(0, hnT[:, 4 + c, :], c, CC)
            last.then_inc(ln_sum, 1)
            for r, bank in ((0, 2), (1, 0)):
                for c in range(CC):
                    pe.wait_ge(ln_sq, r * CC + c + 1)
                    sum_rows(bank, tmp[:, c % 2, :], c, CC).then_inc(ln_used, 1)

            for n in range(NT):
                pe.wait_ge(ao_scaled, n + 1)
                if n >= 2:
                    pe.wait_ge(ao_mixed, n - 1)
                for m in range(4):
                    last = nc.tensor.transpose(ps[:, 4 + n % 2, m * P:(m + 1) * P], o_all[:, n, m * P:(m + 1) * P], ident)
                last.then_inc(ao_t, 1)

            def turn(n):
                pe.wait_ge(h_scaled, n + 1)
                if n >= 2:
                    pe.wait_ge(hnT_ready, n - 1)
                for m in range(DK):
                    last = nc.tensor.transpose(ps[:, 4 + 2 * (n % 2) + m // 4, (m % 4) * P:(m % 4 + 1) * P],
                                               tmp[:, n % 2, m * P:(m + 1) * P], ident)
                last.then_inc(h_t, 1)

            pe.wait_ge(wout_in, 16)
            pe.wait_ge(ln_y, 3 * CC)
            pe.wait_ge(ao_mixed, NT)
            for n in range(NT):
                if n >= 2:
                    pe.wait_ge(h_ready, n - 1)
                for hb in range(2):
                    for m in range(DK):
                        last = mm(ps[:, 2 * (n % 2) + hb, :], hnT[:, m, n * P:(n + 1) * P],
                                  wide[:, m, hb * 512:(hb + 1) * 512], start=m == 0, stop=m == DK - 1)
                last.then_inc(wo_ready, 1)
                if n:
                    turn(n - 1)
            turn(NT - 1)

            def key_scores(c):
                pe.wait_ge(q_copied, c + 1)
                if c >= 2:
                    pe.wait_ge(ks_free, c - 1)
                for n in range(NT):
                    last = mm(ps[:, 4 + 2 * (c % 2) + n // 4, (n % 4) * P:(n % 4 + 1) * P],
                              qc[:, c % 2, n * P:(n + 1) * P], keys[:, c, :], start=True, stop=True)
                last.then_inc(ks_ready, 1)

            pe.wait_ge(hnT_ready, NT)
            pe.wait_ge(h_ready, NT)
            pe.wait_ge(keys_in, 16)
            for c in range(HP):
                pe.wait_ge(wq_in_slot[c % 4], 16 * (c // 4 + 1))
                if c >= 2:
                    pe.wait_ge(q_copied, c - 1)
                for k in range(DK):
                    for hb in range(2):
                        last = mm(ps[:, 2 * (c % 2) + hb, :], wqbuf[:, c % 4, k, :], hnT[:, k, hb * 512:(hb + 1) * 512],
                                  start=k == 0, stop=k == DK - 1)
                last.then_inc(q_ready, 1)
                if c:
                    key_scores(c - 1)
            key_scores(HP - 1)

            pe.wait_ge(ks_free, HP)
            pe.sem_inc(gp_ready, CREDIT)
            with pe.Fori(0, NT) as i:
                pe.wait_ge(sel_ready, i + 1)
                for d in range(3):
                    last = nc.tensor.transpose(ps[:, 5, d * P:(d + 1) * P], sel3[:, d, :], ident)
                last.then_inc(selT_ps, 1)
                with pe.Fori(0, P // (SLOTS * HOT)) as k:
                    for j in range(SLOTS * HQ):
                        e = j % 2
                        quad = i * (P // 4) + k * (SLOTS * HQ) + j
                        b = j // HQ
                        if j % HQ == 0:
                            pe.wait_ge(hot_ready, i * (P // HOT) + k * SLOTS + b + 1)
                        pe.wait_ge(gp_free, quad + 1)
                        for q in range(4):
                            last = mm(ps[:, 6 + e, q * P:(q + 1) * P], hot[:, b, 1, (j % HQ) * 4 + q, :],
                               hot[:, b, 0, (j % HQ) * 4 + q, :],
                                      start=True, stop=True)
                        last.then_inc(gp_ready, 1)

            def group(half, g, first=False):
                G = half * NG + g
                for c in range(GC):
                    n = half * NKEY + g * GC + c
                    pe.wait_ge(ul_ready, n + 1)
                    pe.wait_ge(uh_ready, n + 1)
                    if not first or c >= 2:
                        pe.wait_ge(gelu_ready, n - 1)
                    for k in range(DK):
                        for w, xx in ((uh, xh), (uh, xl), (ul, xh)):
                            last = mm(ps[:, c % 2, :], w[:, c % 2, k, :], xx[:, k, :],
                                      start=k == 0 and w is uh and xx is xh, stop=k == DK - 1 and w is ul)
                    last.then_inc(hp_ready, 1)

                def second(k, cs):
                    tt, dh = k % HT, k // HT
                    for c in cs:
                        for w, v in ((wh, vh), (wh, vl), (wl, vh)):
                            last = mm(ps[:, 2 + k % 4, :], w[:, c, tt * P:(tt + 1) * P], v[:, c, dh * 512:(dh + 1) * 512],
                                      start=c == 0 and w is wh and v is vh, stop=c == GC - 1 and w is wl)
                    return last

                pe.wait_ge(wl_ready, half * NKEY + g * GC + GC - 1)
                for k in range(2):
                    if not first:
                        pe.wait_ge(op_free, G * 8 + k - 3)
                    second(k, range(GC - 1))
                pe.wait_ge(wl_ready, half * NKEY + g * GC + GC)
                for k in range(2):
                    second(k, [GC - 1]).then_inc(op_ready, 1)
                for k in range(2, 8):
                    if not first or k >= 4:
                        pe.wait_ge(op_free, G * 8 + k - 3)
                    second(k, range(GC)).then_inc(op_ready, 1)

            for half in range(2):
                pe.wait_ge(xl_ready, (half + 1) * DK)
                if half == 0:
                    group(0, 0, first=True)
                with pe.Fori(1 - half, NG) as g:
                    group(half, g)


_INS = ["x", "norm_mix_g", "w_in", "conv_w", "conv_b", "conv_ln_g", "conv_ln_b", "attn_sinks", "attn_out_g",
        "conv_out_g", "w_out", "norm_ffn_g", "peer_w_q", "peer_sub_keys", "peer_u", "peer_v", "final_norm_g"]


def constants():
    import numpy as np

    con = np.zeros((P, C_END), np.float32)
    con[:, C_ID:C_ID + P] = np.eye(P)
    con[:, C_ONE:C_ONE + P] = 1
    con[:, C_IOTA:C_IOTA + P] = np.arange(P)
    half = HD // 2
    for m in range(P):
        first = m % HD < half
        con[m + half if first else m - half, C_ROT + m] = -1 if first else 1
    rel = np.arange(P)[:, None] + P - np.arange(2 * P)[None, :]
    band = (rel >= 0) & (rel < P)
    con[:, C_MASK:C_MASK + 2 * P] = np.where(band, 0, NEG)
    con[:, C_MASK0:C_MASK0 + 2 * P] = np.where(band & (np.arange(2 * P)[None, :] >= P), 0, NEG)
    inv = (10000.0 ** (-np.arange(half) / half)).astype(np.float32)
    ang = np.arange(T, dtype=np.float32)[None, :] * inv[:, None]
    con[:, C_COS:C_COS + T] = np.tile(np.cos(ang.astype(np.float64)), (P // half, 1))
    con[:, C_SIN:C_SIN + T] = np.tile(np.sin(ang.astype(np.float64)), (P // half, 1))
    return con


def kernel(**inputs):
    import numpy as np
    import concourse.bacc as bacc
    from concourse.bass_utils import run_bass_kernel_spmd

    a = {k: np.asarray(inputs[k]) for k in _INS}

    def rows(m):
        return m.reshape(m.shape[0] // P, P, -1).transpose(1, 0, 2)

    def cols(v):
        return v.reshape(-1, P).T

    x = a["x"].reshape(T, D)
    w_in = a["w_in"][0]
    q_cols = np.arange(HEADS * HD).reshape(KVH, GQ, HD).transpose(1, 0, 2).reshape(GQ, P)
    blocks = []
    for c in range(CC):
        blocks += [np.arange(768 + c * P, 768 + (c + 1) * P), np.arange(1280 + c * P, 1280 + (c + 1) * P)]
    blocks += [np.arange(512, 640), np.arange(640, 768), *q_cols]
    w_blocks = np.stack([rows(w_in[:, b]) for b in blocks])
    w_q = np.stack([rows(b) for b in np.split(a["peer_w_q"][0], HP, axis=1)])
    keysT = a["peer_sub_keys"][0].reshape(HP, NKEY, P).transpose(2, 0, 1)
    uT = a["peer_u"][0].reshape(NKEY, P, DK, P).transpose(0, 3, 2, 1).reshape(NKEY, P, D)
    v_tab = a["peer_v"][0].reshape(NKEY, P, D)
    conv_w = a["conv_w"][0].T.reshape(CC, P, TAPS).transpose(1, 0, 2).reshape(P, CC * TAPS)
    params = np.concatenate(
        [cols(a["norm_mix_g"][0]), cols(a["norm_ffn_g"][0]), cols(a["attn_out_g"][0]), cols(a["conv_out_g"][0]),
         cols(a["conv_b"][0]), cols(a["conv_ln_g"][0]), cols(a["conv_ln_b"][0]),
         np.tile(a["attn_sinks"][0][None, :], (P, 1)), conv_w, np.full((P, 1), EPS, np.float32)], axis=1)
    data = {"x": x, "xT": rows(np.ascontiguousarray(x.T)), "w_in": w_blocks, "w_out": rows(a["w_out"][0]), "w_q": w_q,
            "keysT": keysT, "uT": uT, "v_tab": v_tab, "consts": constants(), "params": params,
            "final_g": a["final_norm_g"]}

    nc = bacc.Bacc("TRN2", target_bir_lowering=False, num_devices=1)
    arrays, args = {}, []
    for name, v in data.items():
        arrays[f"in_{name}"] = np.ascontiguousarray(v)
        args.append(nc.dram_tensor(f"in_{name}", v.shape, mybir.dt.from_np(v.dtype), kind="ExternalInput").ap())
    args.append(nc.dram_tensor("out_y", (T, D), F32, kind="ExternalOutput").ap())
    decoder_block(nc, *args)
    r = run_bass_kernel_spmd(nc, [arrays], core_ids=[0])
    return r.results[0]["out_y"].reshape(1, T, D)
```

```python
from contextlib import ExitStack

import concourse.bass as bass
from concourse import mybir

P = 128
D = 1024
T = 1024
DK = D // P
NT = T // P
HEADS, KVH, HD = 8, 2, 64
GQ = HEADS // KVH
CONV = 512
CC = CONV // P
TAPS = 31
PH = 8
HP = 2 * PH
NKEY = 128
TOPK = 16
EPS = 1e-6
NEG = -1e30
LOWEST = -3.0e38
HALF = T // 2
HT = HALF // P
SUB = 32
HOT = 8
HQ = HOT // 4
BLOCKS = P // HOT
RAW = 4
ROWS = 2
ROWS_CREDIT = ROWS * HQ
BANKS = 2
WIDE = 4
NCAND = WIDE * TOPK + (TOPK - WIDE) * WIDE
UNITS = 2 * HP
ALONE = 20
SPREAD = 3
MIXED_TILES = 4
STEPS_PICK = 14
EARLY_STEPS = 7
LATE_STEPS = {0: 7, 1: 8, 2: 9, 3: 10, 4: 11, 6: 12, 8: 13}
INDEX_AFTER = (2, 4)
TURN_AFTER = 9
GC = 4
NG = NKEY // GC

CH_GATE, CH_K, CH_V, CH_Q = 0, 8, 9, 10
NCH = 14

C_ID, C_ONE, C_IOTA, C_ROT, C_MASK0, C_MASK, C_COS, C_SIN = 0, 128, 256, 384, 512, 768, 1024, 2048
C_END = 3072
G_MIX, G_FFN, G_ATT, G_CONV, B_CONV, LN_G, LN_B, SINK, CW = 0, 8, 16, 20, 24, 28, 32, 36, 44
G_EPS = CW + CC * TAPS
G_END = G_EPS + 1

F32 = mybir.dt.float32
F32R = mybir.dt.float32r
U32 = mybir.dt.uint32
BF16 = mybir.dt.bfloat16
ALU = mybir.AluOpType
ACT = mybir.ActivationFunctionType
AX = mybir.AxisListType


def decoder_block(nc, x, xT, w_in, w_out, w_q, keysT, uT, v_tab, consts, params, final_g, out):
    gates = nc.dram_tensor("gates", (2, NG, P, HALF // SUB, GC, SUB), F32, kind="Internal").ap()

    ctx = ExitStack()
    early = ExitStack()
    late = ExitStack()

    def sb(name, shape, dt=F32, where=ctx):
        return where.enter_context(nc.sbuf_tensor(name, shape, dt))

    def sem(name):
        return ctx.enter_context(nc.semaphore(name))

    with ctx:
        acc = sb("acc", [P, NT, D])
        hnT = sb("hnT", [P, DK, T])
        con = sb("con", [P, C_COS])
        par = sb("par", [P, G_END])
        small = sb("small", [P, 64])
        ident = con[:, C_ID:C_ID + P]
        ones = con[:, C_ONE:C_ONE + P]
        iota = con[:, C_IOTA:C_IOTA + P]

        rope = sb("rope", [P, 2, T], where=early)
        wide = sb("wide", [P, DK, T], where=early)
        wbuf = sb("wbuf", [P, 4, DK, P], where=early)
        ubuf = sb("ubuf", [P, CC, T + TAPS - 1], where=early)
        tmp = sb("tmp", [P, 2, T], where=early)
        tmp2 = sb("tmp2", [P, T], where=early)
        rb = sb("rb", [P, T], where=early)
        qT = sb("qT", [P, GQ, T], where=early)
        kT = sb("kT", [P, P + T], where=early)
        vv = sb("vv", [P, NT + 1, P], where=early)
        sm = sb("sm", [P, 3, GQ, 2 * P], where=early)
        pT = sb("pT", [P, 2 * GQ, P], where=early)
        att = sb("att", [P, 4, 6, GQ], where=early)
        tap = sb("tap", [P, 2, T], where=early)
        early.close()
        o_all = ubuf[:, :, :].rearrange("p c t -> p (c t)")[:, 0:NT * 512].rearrange("p (n d) -> p n d", n=NT)

        mid = ExitStack()
        s16 = sb("s16", [P, NT, HP, TOPK], where=mid)
        i16 = sb("i16", [P, NT, HP, TOPK], U32, where=mid)
        i16f = i16[:, :, :, :].bitcast(F32)
        wqbuf = sb("wqbuf", [P, 4, DK, P], where=mid)
        keys = sb("keys", [P, HP, NKEY], where=mid)
        qc = sb("qc", [P, 2, HALF], where=mid)
        swork = sb("swork", [P, HT, NKEY], where=mid)
        pick = ExitStack()
        cand = sb("cand", [P, PH, TOPK * TOPK], where=pick)
        cand2 = sb("cand2", [P, PH, TOPK * TOPK], where=pick)
        best = sb("best", [P, PH, TOPK], where=pick)
        bpos = sb("bpos", [P, PH * TOPK], U32, where=pick)
        bdig = sb("bdig", [P, 5, PH * TOPK], U32, where=pick)
        bdigf = bdig[:, :, :].bitcast(F32)
        ranks = sb("ranks", [P, 2, PH * TOPK], where=pick)
        sel3 = sb("sel3", [P, 3, P], where=pick)
        selI = sb("selI", [P, 2, BLOCKS, 2, HOT], BF16, where=pick)
        selG = sb("selG", [P, 2, P], where=pick)
        iota2 = sb("iota2", [P, NKEY, 2], BF16, where=pick)
        marks = sb("marks", [P, RAW, 2, HOT // 2, NKEY, 2], BF16, where=pick)
        hot = sb("hot", [P, ROWS, 2, HOT, P], where=pick)
        den = sb("den", [P, 2, PH], where=pick)
        gbuf = sb("gbuf", [P, 2, NKEY, SUB], where=pick)
        pick.close()
        mid.close()

        xh = sb("xh", [P, DK, HALF], F32R, where=late)
        xl = sb("xl", [P, DK, HALF], F32R, where=late)
        u_raw = sb("u_raw", [P, 2, D], where=late)
        uh = sb("uh", [P, 2, DK, P], F32R, where=late)
        ul = sb("ul", [P, 2, DK, P], F32R, where=late)
        v_raw = sb("v_raw", [P, GC, D], where=late)
        vh = sb("vh", [P, GC, D], F32R, where=late)
        vl = sb("vl", [P, GC, D], F32R, where=late)
        gt = sb("gt", [P, HALF // SUB, GC, SUB], where=late)
        hg = sb("hg", [P, 2, HALF], where=late)
        wh = sb("wh", [P, GC, HALF], F32R, where=late)
        wl = sb("wl", [P, GC, HALF], F32R, where=late)
        late.close()
        fin = ExitStack()
        fg = sb("fg", [P, D], where=fin)
        fo = sb("fo", [P, 2, D], where=fin)
        fscr = sb("fscr", [P, D], where=fin)
        fin.close()

        ps = ctx.enter_context(nc.psum_tensor("ps", [P, 8, 512], F32))

        sq4 = [P, PH, TOPK, TOPK]
        c4 = cand[:, :, :].rearrange("p h (a b) -> p h a b", a=TOPK)
        c4b = cand2[:, :, :].rearrange("p h (a b) -> p h a b", a=TOPK)

        def bank2(b):
            return ps[:, b:b + 2, :].rearrange("p b n -> p (b n)")

        consts_in, rope_in, params_in = sem("consts_in"), sem("rope_in"), sem("params_in")
        xT_in = [sem(f"xT_in{k}") for k in range(DK)]
        x_in = sem("x_in")
        w_in_slot = [sem(f"w_in_slot{k}") for k in range(4)]
        wq_in_slot = [sem(f"wq_in_slot{k}") for k in range(4)]
        wout_in, keys_in = sem("wout_in"), sem("keys_in")
        def sems(names):
            return [sem(n) for n in names.split()]

        pads_ready, sq_ready, sq_used, rms_root, hn_ready = sems("pads_ready sq_ready sq_used rms_root hn_ready")
        proj_ready = sem("proj_ready")
        pair_free = [sem("pair_free0"), sem("pair_free1")]
        raw_ready, rot_ready, rope_done, v_copied = sems("raw_ready rot_ready rope_done v_copied")
        gate_out, conv_dve, conv_pool = sems("gate_out conv_dve conv_pool")
        ln_sum, ln_stat, ln_y, ln_sq, ln_used = sems("ln_sum ln_stat ln_y ln_sq ln_used")
        sc_ready, sm_ready, sc_free, p_ready, pt_ready, pt_copied, o_ready, o_done = sems(
            "sc_ready sm_ready sc_free p_ready pt_ready pt_copied o_ready o_done")
        ao_root, ao_rec, ao_scaled, ao_t, ao_mixed = sems("ao_root ao_rec ao_scaled ao_t ao_mixed")
        wo_ready, h_ready, h_root, h_rec, h_scaled, h_t, hnT_ready = sems(
            "wo_ready h_ready h_root h_rec h_scaled h_t hnT_ready")
        q_ready, q_copied, ks_ready, ks_free = sems("q_ready q_copied ks_ready ks_free")
        best_ready, exp_ready, dig_ready, idx_ready, sel_ready, selT_ps, selT_ready = sems(
            "best_ready exp_ready dig_ready idx_ready sel_ready selT_ps selT_ready")
        hot_eq, hot_plain, hot_scaled, gp_ready, gp_free = sems("hot_eq hot_plain hot_scaled gp_ready gp_free")
        gates_out = [sem("gates_out0"), sem("gates_out1")]
        xh_ready, xl_ready = sem("xh_ready"), sem("xl_ready")
        u_in = [sem(f"u_in{k}") for k in range(2)]
        v_in = [sem(f"v_in{k}") for k in range(GC)]
        g_in = sem("g_in")
        uh_ready, ul_ready, vh_ready, vl_ready = sems("uh_ready ul_ready vh_ready vl_ready")
        hp_ready, gelu_ready, w_ready, wh_ready, wl_ready = sems("hp_ready gelu_ready w_ready wh_ready wl_ready")
        op_ready, op_free = sems("op_ready op_free")
        f_root, f_ready, fg_in = sems("f_root f_ready fg_in")
        f_out = [sem("f_out0"), sem("f_out1")]

        block = ctx.enter_context(nc.Block())
        STEPS = [(n, g) for n in range(NT) for g in range(KVH)]
        NS = len(STEPS)
        PAIR = [0, 2] * (NCH // 2)

        @block.sync
        def _(sp):
            sp.dma_start(con[:, :], consts[:, 0:C_COS]).then_inc(consts_in, 16)
            sp.dma_start(par[:, :], params).then_inc(params_in, 16)
            for k in range(DK):
                sp.dma_start(wide[:, k, :], xT[:, k, :]).then_inc(xT_in[k], 16)
            for c in range(4):
                sp.dma_start(wbuf[:, c, :, :], w_in[c]).then_inc(w_in_slot[c], 16)
            sp.dma_start(rope[:, :, :], consts[:, C_COS:C_END].rearrange("p (s t) -> p s t", s=2)).then_inc(rope_in, 16)
            for c in range(4, NCH):
                sp.wait_ge(proj_ready, c - 3)
                sp.dma_start(wbuf[:, c % 4, :, :], w_in[c]).then_inc(w_in_slot[c % 4], 16)
            sp.dma_start(acc[:, :, :], x.rearrange("(n p) d -> p n d", p=P)).then_inc(x_in, 16)
            sp.wait_ge(proj_ready, NCH)
            sp.dma_start(wide[:, :, :], w_out).then_inc(wout_in, 16)
            sp.wait_ge(wo_ready, NT)
            sp.dma_start(keys[:, :, :], keysT).then_inc(keys_in, 16)

            def load_wq(m):
                if m >= 4:
                    sp.wait_ge(q_ready, m - 3)
                sp.dma_start(wqbuf[:, m % 4, :, :], w_q[m % HP]).then_inc(wq_in_slot[m % 4], 16)

            def write_gates(half, m, s):
                sp.wait_ge(gp_free, (half * (HALF // SUB) + m + 1) * (SUB // 4) + BANKS)
                sp.dma_start(gates[half, :, :, m, :, :].rearrange("g p c t -> p g (c t)") if isinstance(m, int) else
                             gates[half, :, :, bass.ds(m, 1), :, :].rearrange("g p o c t -> p g (o c t)"),
                             gbuf[:, s, :, :].rearrange("p (g c) t -> p g (c t)", c=GC)).then_inc(gates_out[s], 16)

            for m in range(ALONE + 4):
                load_wq(m)
            for n in range(MIXED_TILES * BLOCKS):
                unit = ALONE + n // SPREAD
                if n % SPREAD == SPREAD - 1 and unit + 4 < UNITS:
                    load_wq(unit + 4)
                if n % (SUB // HOT) == SUB // HOT - 1:
                    write_gates(0, n * HOT // SUB, n * HOT // SUB % 2)
            with sp.Fori(0, HALF // SUB // 2) as i:
                for s in range(2):
                    write_gates(1, i * 2 + s, s)
            for b in range(2):
                sp.wait_ge(gates_out[b], 16 * (T // SUB // 2))

            def load_gates(half, g):
                sp.dma_start(gt[:, :, :, :], gates[half, g]).then_inc(g_in, 16)

            def load_group(half, g, first=False):
                for c in range(GC):
                    n = half * NKEY + g * GC + c
                    if not first or c >= 2:
                        sp.wait_ge(uh_ready, n - 1)
                        sp.wait_ge(ul_ready, n - 1)
                    sp.dma_start(u_raw[:, c % 2, :], uT[g * GC + c]).then_inc(u_in[c % 2], 16)
                    if not first:
                        sp.wait_ge(vh_ready, n - GC + 1)
                        sp.wait_ge(vl_ready, n - GC + 1)
                    sp.dma_start(v_raw[:, c, :], v_tab[g * GC + c]).then_inc(v_in[c], 16)
                    if first and c == 0:
                        load_gates(half, g)
                if not first:
                    sp.wait_ge(w_ready, half * NKEY + g * GC)
                    load_gates(half, g)

            load_group(0, 0, first=True)
            with sp.Fori(1, NG) as g:
                load_group(0, g)
            with sp.Fori(0, NG) as g:
                load_group(1, g)
            sp.wait_ge(op_free, 2 * NG * 8)
            sp.dma_start(fg[:, :], final_g.partition_broadcast(P)).then_inc(fg_in, 16)
            for n in range(NT):
                sp.wait_ge(f_ready, n + 1)
                sp.dma_start(out[n * P:(n + 1) * P, :], fo[:, n % 2, :]).then_inc(f_out[n % 2], 16)
            for b in range(2):
                sp.wait_ge(f_out[b], 16 * (NT // 2))

        @block.gpsimd
        def _(pool):
            nc.gpsimd.memset(ubuf[:, :, 0:TAPS - 1], 0.0)
            nc.gpsimd.memset(kT[:, 0:P], 0.0)
            nc.gpsimd.memset(vv[:, 0, :], 0.0).then_inc(pads_ready, 1)
            pool.wait_ge(pads_ready, 1)
            for c in (0, CC - 1):
                u, y = ubuf[:, c, TAPS - 1:], hnT[:, 4 + c, :]
                pool.wait_ge(gate_out, 2 * c + 2)
                nc.gpsimd.tensor_tensor(u, u, y, ALU.mult)
                pool.drain()
                nc.gpsimd.tensor_scalar(y, ubuf[:, c, 0:T], par[:, CW + c * TAPS:CW + c * TAPS + 1],
                                        par[:, B_CONV + c:B_CONV + c + 1], ALU.mult, ALU.add)
                for k in range(1, TAPS):
                    nc.gpsimd.tensor_scalar(tap[:, k % 2, :], ubuf[:, c, k:k + T],
                                            par[:, CW + c * TAPS + k:CW + c * TAPS + k + 1], 0.0, ALU.mult, ALU.add)
                    pool.drain()
                    nc.gpsimd.tensor_tensor(y, y, tap[:, k % 2, :], ALU.add)
                pool.drain()
                pool.sem_inc(conv_pool, 1)

            pool.sem_inc(hot_scaled, RAW)

            def index(i, d):
                it = i16f[:, bass.ds(i, 1) if not isinstance(i, int) else slice(i, i + 1), :, :].rearrange("p o (h s) k -> p (o h) s k", s=2)
                cc = (c4, c4b)[d]
                pool.wait_ge(dig_ready, i * 2 + d + 1)
                nc.gpsimd.tensor_tensor(cc, cc, it[:, :, d, :].unsqueeze(2).to_broadcast(sq4), ALU.mult).then_inc(idx_ready, 1)

            def tile(i, u, ahead=2):
                for b in range(BLOCKS):
                    n = i * BLOCKS + b
                    pool.wait_ge(hot_eq, n + 1)
                    pool.wait_ge(gp_ready, (n + 1) * HQ)
                    gate = selG[:, u, b * HOT:(b + 1) * HOT].rearrange("p (c e) -> p c e", e=2)
                    nc.gpsimd.tensor_tensor(hot[:, b % ROWS, 1, :, :].rearrange("p (c e) k -> p c e k", e=2),
                                            marks[:, b % RAW, 1, :, :, :].rearrange("p c k e -> p c e k"),
                                            gate.unsqueeze(3).to_broadcast([P, HOT // 2, 2, NKEY]),
                                            ALU.mult).then_inc(hot_scaled, 1)
                    if ahead and b in INDEX_AFTER:
                        index(i + 1, INDEX_AFTER.index(b))

            for d in range(2):
                index(0, d)
            with pool.Fori(0, NT // 2 - 1) as j:
                for u in range(2):
                    tile(j * 2 + u, u)
            tile(NT - 2, 0, ahead=1)
            tile(NT - 1, 1, ahead=0)

        @block.scalar
        def _(act):
            for k in range(DK):
                act.wait_ge(xT_in[k], 16)
                if k >= 2:
                    act.wait_ge(sq_used, k - 1)
                nc.scalar.activation(tmp[:, k % 2, :], wide[:, k, :], ACT.Square).then_inc(sq_ready, 1)
            act.wait_ge(sq_used, DK)
            act.wait_ge(params_in, 16)
            nc.scalar.activation(rb[:, :], bank2(0), ACT.Sqrt, bias=par[:, G_EPS:G_END], scale=1.0 / D).then_inc(rms_root, 1)

            def copy_raw(r, blk):
                act.wait_ge(proj_ready, blk + 1)
                if r >= 2:
                    act.wait_ge(rope_done, r - 1)
                nc.scalar.copy(tmp[:, r % 2, :], bank2(2 * (blk % 2))).then_inc(raw_ready, 1)

            for c in range(CC):
                act.wait_ge(proj_ready, CH_GATE + 2 * c + 1)
                nc.scalar.copy(ubuf[:, c, TAPS - 1:], bank2(0)).then_inc(gate_out, 1)
                act.wait_ge(proj_ready, CH_GATE + 2 * c + 2)
                nc.scalar.activation(hnT[:, 4 + c, :], bank2(2), ACT.Sigmoid).then_inc(gate_out, 1)
            copy_raw(0, CH_K)
            act.wait_ge(proj_ready, CH_V + 1)
            nc.scalar.copy(vv[:, 1:NT + 1, :].rearrange("p n d -> p (n d)"), bank2(2 * (CH_V % 2))).then_inc(v_copied, 1)
            for j in range(GQ):
                copy_raw(1 + j, CH_Q + j)

            def probs(s):
                act.wait_ge(sm_ready, s + 1)
                for j in range(GQ):
                    nc.scalar.activation(sm[:, s % 3, j, :], sm[:, s % 3, j, :], ACT.Exp, bias=att[:, s % 4, 1, j:j + 1],
                                         accum_out=att[:, s % 4, 3, j:j + 1])
                nc.scalar.activation(att[:, s % 4, 4, :], att[:, s % 4, 2, :], ACT.Exp).then_inc(p_ready, 1)

            for s in range(NS + 1):
                if s < NS:
                    probs(s)
                if s:
                    act.wait_ge(pt_ready, s)
                    if s >= 2:
                        act.wait_ge(o_ready, s - 1)
                    nc.scalar.copy(pT[:, :, :].rearrange("p j q -> p (j q)"), bank2(4)).then_inc(pt_copied, 1)

            act.wait_ge(ln_sum, 1)
            nc.scalar.mul(rb[:, :], bank2(0), 1.0 / CONV).then_inc(ln_stat, 1)

            def squares(c, k, waits):
                act.wait_ge(ln_y, waits)
                if k >= 2:
                    act.wait_ge(ln_used, k - 1)
                nc.scalar.activation(tmp[:, k % 2, :], hnT[:, 4 + c, :], ACT.Square).then_inc(ln_sq, 1)

            for c in range(CC):
                squares(c, c, c + 1)
            act.wait_ge(ln_used, CC)
            nc.scalar.activation(rb[:, :], bank2(2), ACT.Sqrt, bias=par[:, G_EPS:G_END], scale=1.0 / CONV).then_inc(ln_stat, 1)
            for c in range(CC):
                act.wait_ge(ln_y, CC + c + 1)
                y = hnT[:, 4 + c, :]
                nc.scalar.activation(y, y, ACT.Silu, bias=par[:, LN_B + c:LN_B + c + 1], scale=par[:, LN_G + c:LN_G + c + 1])
                act.drain()
                if CC + c >= 2:
                    act.wait_ge(ln_used, CC + c - 1)
                nc.scalar.activation(tmp[:, c % 2, :], y, ACT.Square).then_inc(ln_sq, 1)
            act.wait_ge(ln_used, 2 * CC)
            nc.scalar.activation(rb[:, :], bank2(0), ACT.Sqrt, bias=par[:, G_EPS:G_END], scale=1.0 / CONV).then_inc(ln_stat, 1)

            for n in range(NT):
                act.wait_ge(o_done, 2 * n + 2)
                nc.scalar.activation(tmp2[:, 0:512], o_all[:, n, :], ACT.Square, accum_out=small[:, n:n + 1])
                act.drain()
            nc.scalar.activation(small[:, 8:16], small[:, 0:8], ACT.Sqrt, bias=par[:, G_EPS:G_END],
                                 scale=1.0 / 512).then_inc(ao_root, 1)
            act.wait_ge(ao_rec, 1)
            for n in range(NT):
                nc.scalar.mul(o_all[:, n, :], o_all[:, n, :], small[:, 16 + n:17 + n]).then_inc(ao_scaled, 1)

            def root(n):
                act.wait_ge(h_ready, n + 1)
                nc.scalar.activation(tmp2[:, :], acc[:, n, :], ACT.Square, accum_out=small[:, 24 + n:25 + n])
                act.drain()
                nc.scalar.activation(small[:, 32 + n:33 + n], small[:, 24 + n:25 + n], ACT.Sqrt,
                                     bias=par[:, G_EPS:G_END], scale=1.0 / D).then_inc(h_root, 1)

            for n in range(NT):
                root(n)
                act.wait_ge(h_rec, n + 1)
                if n >= 2:
                    act.wait_ge(h_t, n - 1)
                nc.scalar.mul(tmp[:, n % 2, :], acc[:, n, :], small[:, 40 + n:41 + n]).then_inc(h_scaled, 1)

            def copy_query(m):
                act.wait_ge(q_ready, m + 1)
                if m >= 2:
                    act.wait_ge(ks_ready, m - 1)
                nc.scalar.copy(qc[:, m % 2, :], ps[:, m % 2, :]).then_inc(q_copied, 1)

            def exps(i):
                act.wait_ge(best_ready, i + 1)
                nc.scalar.activation(best[:, :, :], best[:, :, :], ACT.Exp).then_inc(exp_ready, 1)

            def selected(i, u):
                act.wait_ge(selT_ps, i + 1)
                nc.scalar.copy(selI[:, u, :, :, :], ps[:, 5, 0:2 * P].rearrange("p (d b t) -> p b d t", d=2, b=BLOCKS))
                nc.scalar.copy(selG[:, u, :], ps[:, 5, 2 * P:3 * P]).then_inc(selT_ready, 1)

            def plain(i, b):
                n = i * BLOCKS + b
                act.wait_ge(hot_eq, n + 1)
                act.wait_ge(gp_ready, (n + 1) * HQ)
                nc.scalar.copy(hot[:, b % ROWS, 0, :, :].rearrange("p (c e) k -> p c e k", e=2),
                               marks[:, b % RAW, 0, :, :, :].rearrange("p c k e -> p c e k")).then_inc(hot_plain, 1)

            def gather(i, b):
                m = b * HOT // SUB
                s = m % 2
                if b * HOT % SUB == 0:
                    act.wait_ge(gates_out[s], (i * (P // SUB // 2) + m // 2) * 16)
                for e in range(HQ):
                    t0 = b * HOT % SUB + e * 4
                    act.wait_ge(gp_ready, (i * BLOCKS + b) * HQ + e + 1 + ROWS_CREDIT)
                    nc.scalar.copy(gbuf[:, s, :, t0:t0 + 4].rearrange("p i t -> p t i"),
                                   ps[:, 6 + e, :].rearrange("p (t i) -> p t i", t=4)).then_inc(gp_free, 1)

            def tile(i, u, ahead=2, mixed=False):
                for b in range(BLOCKS):
                    if mixed:
                        unit = ALONE + (i * BLOCKS + b) // SPREAD
                        if (i * BLOCKS + b) % SPREAD == 0 and ALONE < unit <= UNITS:
                            copy_query(unit - 1)
                    plain(i, b)
                    if b:
                        gather(i, b - 1)
                    if ahead and b == 1:
                        exps(i + 1)
                    if ahead and b == TURN_AFTER + 1:
                        selected(i + 1, 1 - u)
                gather(i, BLOCKS - 1)

            for m in range(ALONE):
                copy_query(m)
                if m == HP + 1:
                    act.sem_inc(gp_free, BANKS)
                    act.sem_inc(hot_plain, RAW)
                    exps(0)
            selected(0, 0)
            for i in range(MIXED_TILES):
                tile(i, i % 2, mixed=True)
            with act.Fori(MIXED_TILES // 2, NT // 2 - 1) as j:
                for u in range(2):
                    tile(j * 2 + u, u)
            tile(NT - 2, 0, ahead=1)
            tile(NT - 1, 1, ahead=0)

            for b in range(2):
                act.wait_ge(gates_out[b], 16 * (T // SUB // 2))

            def split_u(half, g, c):
                act.wait_ge(u_in[c % 2], 16 * (half * (NKEY // 2) + g * (GC // 2) + c // 2 + 1))
                nc.scalar.copy(uh[:, c % 2, :, :].rearrange("p k e -> p (k e)"), u_raw[:, c % 2, :]).then_inc(uh_ready, 1)

            def group(half, g, first=False, last=False):
                n0 = half * NKEY + g * GC
                if not first:
                    act.wait_ge(op_ready, (half * NG + g) * 8)
                for c in range(GC):
                    n = n0 + c
                    act.wait_ge(v_in[c], 16 * (half * NG + g + 1))
                    nc.scalar.copy(vh[:, c, :], v_raw[:, c, :]).then_inc(vh_ready, 1)
                    act.wait_ge(hp_ready, n + 1)
                    if not first or c >= 2:
                        act.wait_ge(wl_ready, n - 1)
                    nc.scalar.activation(hg[:, c % 2, :], ps[:, c % 2, :], ACT.Gelu).then_inc(gelu_ready, 1)
                    act.wait_ge(w_ready, n + 1)
                    nc.scalar.copy(wh[:, c, :], hg[:, c % 2, :]).then_inc(wh_ready, 1)
                    if c < 2:
                        split_u(half, g, c + 2)
                    elif not last:
                        split_u(half, g + 1, c - 2)

            for half in range(2):
                if half:
                    act.wait_ge(hp_ready, NKEY)
                for k in range(DK):
                    nc.scalar.copy(xh[:, k, :], hnT[:, k, half * HALF:(half + 1) * HALF]).then_inc(xh_ready, 1)
                split_u(half, 0, 0)
                split_u(half, 0, 1)
                if half == 0:
                    group(0, 0, first=True)
                with act.Fori(1 - half, NG - 1) as g:
                    group(half, g)
                group(half, NG - 1, last=True)

            act.wait_ge(op_free, 2 * NG * 8)
            for n in range(NT):
                nc.scalar.activation(fscr[:, :], acc[:, n, :], ACT.Square, accum_out=small[:, n:n + 1])
                act.drain()
            nc.scalar.activation(small[:, 8:16], small[:, 0:8], ACT.Sqrt, bias=par[:, G_EPS:G_END],
                                 scale=1.0 / D).then_inc(f_root, 1)

        @block.vector
        def _(dve):
            dve.wait_ge(rms_root, 1)
            nc.vector.reciprocal(rb[:, :], rb[:, :])
            dve.drain()
            for k in range(DK):
                nc.vector.scalar_tensor_tensor(out=wide[:, k, :], in0=wide[:, k, :], scalar=par[:, G_MIX + k:G_MIX + k + 1],
                                               in1=rb[:, :], op0=ALU.mult, op1=ALU.mult).then_inc(hn_ready, 1)

            dve.wait_ge(pads_ready, 1)
            for c in range(1, CC - 1):
                y = hnT[:, 4 + c, :]
                u = ubuf[:, c, TAPS - 1:]
                dve.wait_ge(gate_out, 2 * c + 2)
                nc.vector.tensor_tensor(u, u, y, ALU.mult)
                dve.drain()
                nc.vector.tensor_scalar(y, ubuf[:, c, 0:T], par[:, CW + c * TAPS:CW + c * TAPS + 1],
                                        par[:, B_CONV + c:B_CONV + c + 1], ALU.mult, ALU.add)
                dve.drain()
                with dve.Fori(0, (TAPS - 1) // 5) as r:
                    for j in range(5):
                        k = r * 5 + j + 1
                        nc.vector.scalar_tensor_tensor(out=y, in0=ubuf[:, c, bass.ds(k, T)],
                                                       scalar=par[:, bass.ds(k + CW + c * TAPS, 1)], in1=y,
                                                       op0=ALU.mult, op1=ALU.add)
                        dve.drain()
                dve.sem_inc(conv_dve, 1)

            dve.wait_ge(rope_in, 16)
            for r in range(1 + GQ):
                dst = kT[:, P:P + T] if r == 0 else qT[:, r - 1, :]
                dve.wait_ge(raw_ready, r + 1)
                nc.vector.tensor_tensor(dst, tmp[:, r % 2, :], rope[:, 0, :], ALU.mult)
                dve.wait_ge(rot_ready, r + 1)
                nc.vector.tensor_tensor(tmp2[:, :], bank2(4), rope[:, 1, :], ALU.mult)
                dve.drain()
                nc.vector.tensor_tensor(dst, dst, tmp2[:, :], ALU.add).then_inc(rope_done, 1)

            def soft(s):
                n, g = STEPS[s]
                b, m = s % 4, s % 3
                mask = con[:, C_MASK0:C_MASK0 + 2 * P] if n == 0 else con[:, C_MASK:C_MASK + 2 * P]
                sink = par[:, SINK + g * GQ:SINK + (g + 1) * GQ]
                dve.wait_ge(sc_ready, s + 1)
                if s >= 3:
                    dve.wait_ge(pt_ready, s - 2)
                nc.vector.scalar_tensor_tensor(
                    out=sm[:, m, :, :], in0=bank2(2 * (s % 2)).rearrange("p (j k) -> p j k", j=GQ), scalar=float(HD) ** -0.5,
                    in1=mask.unsqueeze(1).to_broadcast([P, GQ, 2 * P]), op0=ALU.mult, op1=ALU.add).then_inc(sc_free, 1)
                dve.drain()
                nc.vector.tensor_reduce(att[:, b, 0, :], sm[:, m, :, :], AX.X, ALU.max)
                dve.drain()
                nc.vector.tensor_tensor(att[:, b, 0, :], att[:, b, 0, :], sink, ALU.max)
                dve.drain()
                nc.vector.tensor_scalar(att[:, b, 1, :], att[:, b, 0, :], -1.0, None, ALU.mult)
                nc.vector.tensor_tensor(att[:, b, 2, :], sink, att[:, b, 0, :], ALU.subtract).then_inc(sm_ready, 1)

            def weighted(s):
                n, g = STEPS[s]
                b = s % 4
                dve.wait_ge(o_ready, s + 1)
                nc.vector.tensor_tensor(att[:, b, 3, :], att[:, b, 3, :], att[:, b, 4, :], ALU.add)
                dve.drain()
                nc.vector.reciprocal(att[:, b, 5, :], att[:, b, 3, :])
                dve.drain()
                if s == 0:
                    dve.wait_ge(conv_pool, 1)
                if s == 2 * 6:
                    dve.wait_ge(conv_pool, 2)
                nc.vector.tensor_tensor(
                    o_all[:, n, g * 256:(g + 1) * 256].rearrange("p (j d) -> p j d", j=GQ),
                    ps[:, 6 + s % 2, 0:256].rearrange("p (j d) -> p j d", j=GQ),
                    att[:, b, 5, :].unsqueeze(2).to_broadcast([P, GQ, HD]), ALU.mult).then_inc(o_done, 1)

            for s in range(NS + 2):
                if s < NS:
                    soft(s)
                if s >= 2:
                    weighted(s - 2)

            dve.wait_ge(ln_stat, 1)
            for c in range(CC):
                y = hnT[:, 4 + c, :]
                nc.vector.tensor_tensor(y, y, rb[:, :], ALU.subtract).then_inc(ln_y, 1)
            dve.wait_ge(ln_stat, 2)
            nc.vector.reciprocal(rb[:, :], rb[:, :])
            dve.drain()
            for c in range(CC):
                y = hnT[:, 4 + c, :]
                nc.vector.tensor_tensor(y, y, rb[:, :], ALU.mult).then_inc(ln_y, 1)
            dve.wait_ge(ln_stat, 3)
            nc.vector.reciprocal(rb[:, :], rb[:, :])
            dve.drain()
            for c in range(CC):
                y = hnT[:, 4 + c, :]
                nc.vector.scalar_tensor_tensor(out=y, in0=y, scalar=par[:, G_CONV + c:G_CONV + c + 1], in1=rb[:, :],
                                               op0=ALU.mult, op1=ALU.mult).then_inc(ln_y, 1)

            dve.wait_ge(ao_root, 1)
            nc.vector.reciprocal(small[:, 16:24], small[:, 8:16]).then_inc(ao_rec, 1)
            for n in range(NT):
                dve.wait_ge(ao_t, n + 1)
                nc.vector.tensor_tensor(
                    hnT[:, 0:4, n * P:(n + 1) * P], ps[:, 4 + n % 2, :].rearrange("p (m t) -> p m t", m=4),
                    par[:, G_ATT:G_ATT + 4].unsqueeze(2).to_broadcast([P, 4, P]), ALU.mult).then_inc(ao_mixed, 1)

            def normed(n):
                dve.wait_ge(h_t, n + 1)
                nc.vector.tensor_tensor(
                    hnT[:, :, n * P:(n + 1) * P], bank2(4 + 2 * (n % 2)).rearrange("p (m t) -> p m t", m=DK),
                    par[:, G_FFN:G_FFN + DK].unsqueeze(2).to_broadcast([P, DK, P]), ALU.mult).then_inc(hnT_ready, 1)

            dve.wait_ge(x_in, 16)
            for n in range(NT):
                dve.wait_ge(wo_ready, n + 1)
                nc.vector.tensor_tensor(acc[:, n, :], acc[:, n, :], bank2(2 * (n % 2)), ALU.add).then_inc(h_ready, 1)
                if n:
                    normed(n - 1)
                dve.wait_ge(h_root, n + 1)
                nc.vector.reciprocal(small[:, 40 + n:41 + n], small[:, 32 + n:33 + n]).then_inc(h_rec, 1)
            normed(NT - 1)

            def scan(m, part):
                c, t0 = m % HP, m // HP * HT
                sv = ps[:, 2 + m % 2, :].rearrange("p (n k) -> p n k", n=HT)
                if part == 0:
                    dve.wait_ge(ks_ready, m + 1)
                    for n in range(HT):
                        nc.vector.max(s16[:, t0 + n, c, 0:8], sv[:, n, :])
                elif part == 1:
                    dve.drain()
                    for n in range(HT):
                        nc.vector.max_index(i16[:, t0 + n, c, 0:8], s16[:, t0 + n, c, 0:8], sv[:, n, :])
                    for n in range(HT):
                        last = nc.vector.match_replace(swork[:, n, :], s16[:, t0 + n, c, 0:8], sv[:, n, :], LOWEST)
                    last.then_inc(ks_free, 1)
                else:
                    dve.drain()
                    for n in range(HT):
                        nc.vector.max(s16[:, t0 + n, c, 8:16], swork[:, n, :])
                    dve.drain()
                    for n in range(HT):
                        nc.vector.max_index(i16[:, t0 + n, c, 8:16], s16[:, t0 + n, c, 8:16], swork[:, n, :])
                    if c == HP - 1:
                        dve.drain()
                        nc.vector.tensor_copy(i16f[:, t0:t0 + HT, :, :].rearrange("p n h k -> p (n h k)"),
                                              i16[:, t0:t0 + HT, :, :].rearrange("p n h k -> p (n h k)"))

            nc.vector.tensor_copy(iota2[:, :, :], iota.unsqueeze(2).to_broadcast([P, NKEY, 2]))

            def pick(i, step):
                if step == 0:
                    dve.drain()
                    st = s16[:, bass.ds(i, 1) if not isinstance(i, int) else slice(i, i + 1), :, :].rearrange("p o (h s) k -> p (o h) s k", s=2)
                    for a0, na, nb in ((0, WIDE, TOPK), (WIDE, TOPK - WIDE, WIDE)):
                        o = a0 * TOPK
                        nc.vector.tensor_tensor(cand[:, :, o:o + na * nb].rearrange("p h (a b) -> p h a b", a=na),
                                                st[:, :, 0, a0:a0 + na].unsqueeze(3).to_broadcast([P, PH, na, nb]),
                                                st[:, :, 1, 0:nb].unsqueeze(2).to_broadcast([P, PH, na, nb]), ALU.add)
                elif step == 1:
                    dve.drain()
                    for h in range(PH):
                        nc.vector.max(best[:, h, 0:8], cand[:, h, 0:NCAND])
                elif step == 2:
                    dve.drain()
                    for h in range(PH):
                        nc.vector.max_index(bpos[:, h * TOPK:h * TOPK + 8], best[:, h, 0:8], cand[:, h, 0:NCAND])
                elif step == 3:
                    for h in range(PH):
                        nc.vector.match_replace(cand2[:, h, 0:NCAND], best[:, h, 0:8], cand[:, h, 0:NCAND], LOWEST)
                elif step == 4:
                    dve.drain()
                    for h in range(PH):
                        nc.vector.max(best[:, h, 8:16], cand2[:, h, 0:NCAND])
                elif step == 5:
                    dve.drain()
                    for h in range(PH):
                        nc.vector.max_index(bpos[:, h * TOPK + 8:h * TOPK + 16], best[:, h, 8:16], cand2[:, h, 0:NCAND])
                    nc.vector.tensor_copy(den[:, 0, :], best[:, :, 0])
                elif step == 6:
                    dve.drain()
                    nc.vector.tensor_tensor(best[:, :, :], best[:, :, :],
                                            den[:, 0, :].unsqueeze(2).to_broadcast([P, PH, TOPK]),
                                            ALU.subtract).then_inc(best_ready, 1)
                    for k, (op, by) in enumerate(((ALU.logical_shift_right, 4), (ALU.logical_shift_right, 2),
                                                  (ALU.bitwise_and, WIDE - 1), (ALU.bitwise_and, TOPK - 1),
                                                  (ALU.logical_shift_right, 6))):
                        nc.vector.tensor_scalar(bdig[:, k, :], bpos[:, :], by, None, op)
                    dve.drain()
                    nc.vector.tensor_copy(bdigf, bdig[:, :, :])
                elif step == 7:
                    dve.drain()
                    nc.vector.scalar_tensor_tensor(out=ranks[:, 0, :], in0=bdigf[:, 1, :], scalar=-12.0, in1=bdigf[:, 0, :],
                                                   op0=ALU.add, op1=ALU.max)
                    nc.vector.scalar_tensor_tensor(out=ranks[:, 1, :], in0=bdigf[:, 4, :], scalar=-16.0, in1=bdigf[:, 3, :],
                                                   op0=ALU.mult, op1=ALU.add)
                    dve.drain()
                    nc.vector.tensor_tensor(ranks[:, 1, :], ranks[:, 1, :], bdigf[:, 2, :], ALU.max)
                elif step in (8, 9):
                    if step == 8:
                        dve.drain()
                    rank = ranks[:, step - 8, :].rearrange("p (h k) -> p h k", h=PH)
                    nc.vector.tensor_tensor((c4, c4b)[step - 8], rank.unsqueeze(3).to_broadcast(sq4),
                                            iota[:, 0:TOPK].unsqueeze(1).unsqueeze(1).to_broadcast(sq4),
                                            ALU.is_equal).then_inc(dig_ready, 1)
                elif step == 10:
                    dve.wait_ge(exp_ready, i + 1)
                    nc.vector.tensor_reduce(den[:, 1, :], best[:, :, :], AX.X, ALU.add)
                    dve.drain()
                    nc.vector.reciprocal(den[:, 0, :], den[:, 1, :])
                elif step == 11:
                    dve.drain()
                    nc.vector.tensor_tensor(sel3[:, 2, :].rearrange("p (h k) -> p h k", h=PH), best[:, :, :],
                                            den[:, 0, :].unsqueeze(2).to_broadcast([P, PH, TOPK]), ALU.mult)
                elif step in (12, 13):
                    d = step - 12
                    dve.wait_ge(idx_ready, i * 2 + d + 1)
                    last = nc.vector.tensor_reduce(sel3[:, d, :].rearrange("p (h k) -> p h k", h=PH), (c4, c4b)[d],
                                                   AX.X, ALU.add)
                    if d:
                        last.then_inc(sel_ready, 1)

            def tile(i, u, ahead=2, mixed=False):
                dve.wait_ge(selT_ready, i + 1)
                for b in range(BLOCKS):
                    dve.wait_ge(hot_plain, i * BLOCKS + b + 1)
                    dve.wait_ge(hot_scaled, i * BLOCKS + b + 1)
                    nc.vector.tensor_tensor(
                        marks[:, b % RAW, :, :, :, :].rearrange("p d c k e -> p (d c) k e"),
                        selI[:, u, b, :, :].rearrange("p d (c e) -> p (d c) e", e=2).unsqueeze(2)
                        .to_broadcast([P, HOT, NKEY, 2]),
                        iota2[:, :, :].unsqueeze(1).to_broadcast([P, HOT, NKEY, 2]), ALU.is_equal).then_inc(hot_eq, 1)
                    if mixed:
                        n = i * BLOCKS + b
                        if ALONE + n // SPREAD - 2 < UNITS:
                            scan(ALONE + n // SPREAD - 2, n % SPREAD)
                    if ahead and b in LATE_STEPS:
                        pick(i + 1, LATE_STEPS[b])
                    if ahead > 1 and b >= BLOCKS - EARLY_STEPS:
                        pick(i + 2, b - (BLOCKS - EARLY_STEPS))

            for m in range(HP):
                for part in range(3):
                    scan(m, part)
            for step in range(10):
                pick(0, step)
            for m in range(HP, ALONE - 2):
                for part in range(3):
                    scan(m, part)
            for step in range(10, STEPS_PICK):
                pick(0, step)
            for step in range(EARLY_STEPS):
                pick(1, step)
            for i in range(MIXED_TILES):
                tile(i, i % 2, mixed=True)
            with dve.Fori(MIXED_TILES // 2, NT // 2 - 1) as j:
                for u in range(2):
                    tile(j * 2 + u, u)
            tile(NT - 2, 0, ahead=1)
            tile(NT - 1, 1, ahead=0)

            def low_u(half, g, c):
                n = half * NKEY + g * GC + c
                dve.wait_ge(uh_ready, n + 1)
                nc.vector.tensor_tensor(ul[:, c % 2, :, :].rearrange("p k e -> p (k e)"), u_raw[:, c % 2, :],
                                        uh[:, c % 2, :, :].rearrange("p k e -> p (k e)").bitcast(F32),
                                        ALU.subtract).then_inc(ul_ready, 1)

            def group(half, g, first=False, last=False):
                n0 = half * NKEY + g * GC
                for c in range(GC):
                    n = n0 + c
                    dve.wait_ge(vh_ready, n + 1)
                    nc.vector.tensor_tensor(vl[:, c, :], v_raw[:, c, :], vh[:, c, :].bitcast(F32),
                                            ALU.subtract).then_inc(vl_ready, 1)
                    if c == 0:
                        dve.wait_ge(g_in, 16 * (half * NG + g + 1))
                    dve.wait_ge(gelu_ready, n + 1)
                    nc.vector.tensor_tensor(hg[:, c % 2, :].rearrange("p (s t) -> p s t", t=SUB),
                                            hg[:, c % 2, :].rearrange("p (s t) -> p s t", t=SUB),
                                            gt[:, :, c, :], ALU.mult).then_inc(w_ready, 1)
                    dve.wait_ge(wh_ready, n + 1)
                    nc.vector.tensor_tensor(wl[:, c, :], hg[:, c % 2, :], wh[:, c, :].bitcast(F32),
                                            ALU.subtract).then_inc(wl_ready, 1)
                    if c < 2:
                        low_u(half, g, c + 2)
                    elif not last:
                        low_u(half, g + 1, c - 2)
                for k in range(8):
                    dve.wait_ge(op_ready, (half * NG + g) * 8 + k + 1)
                    dst = acc[:, half * HT + k % HT, (k // HT) * 512:(k // HT + 1) * 512]
                    nc.vector.tensor_tensor(dst, dst, ps[:, 2 + k % 4, :], ALU.add).then_inc(op_free, 1)

            for half in range(2):
                for k in range(DK):
                    dve.wait_ge(xh_ready, half * DK + k + 1)
                    nc.vector.tensor_tensor(xl[:, k, :], hnT[:, k, half * HALF:(half + 1) * HALF],
                                            xh[:, k, :].bitcast(F32), ALU.subtract).then_inc(xl_ready, 1)
                low_u(half, 0, 0)
                low_u(half, 0, 1)
                if half == 0:
                    group(0, 0, first=True)
                with dve.Fori(1 - half, NG - 1) as g:
                    group(half, g)
                group(half, NG - 1, last=True)

            dve.wait_ge(f_root, 1)
            nc.vector.reciprocal(small[:, 16:24], small[:, 8:16])
            dve.drain()
            dve.wait_ge(fg_in, 16)
            for n in range(NT):
                if n >= 2:
                    dve.wait_ge(f_out[n % 2], 16 * (n // 2))
                nc.vector.scalar_tensor_tensor(out=fo[:, n % 2, :], in0=acc[:, n, :], scalar=small[:, 16 + n:17 + n],
                                               in1=fg[:, :], op0=ALU.mult, op1=ALU.mult).then_inc(f_ready, 1)

        @block.tensor
        def _(pe):
            mm = nc.tensor.matmul
            pe.wait_ge(consts_in, 16)

            def sum_rows(bank, src, k, n):
                for hb in range(2):
                    last = mm(ps[:, bank + hb, :], ones, src[:, hb * 512:(hb + 1) * 512], start=k == 0, stop=k == n - 1)
                return last

            for k in range(DK):
                pe.wait_ge(sq_ready, k + 1)
                sum_rows(0, tmp[:, k % 2, :], k, DK).then_inc(sq_used, 1)

            def rotate(r):
                pe.wait_ge(raw_ready, r + 1)
                if r:
                    pe.wait_ge(rope_done, r)
                for hb in range(2):
                    last = mm(ps[:, 4 + hb, :], con[:, C_ROT:C_ROT + P], tmp[:, r % 2, hb * 512:(hb + 1) * 512],
                              start=True, stop=True)
                last.then_inc(rot_ready, 1)

            pe.wait_ge(rms_root, 1)
            for blk in range(NCH):
                pe.wait_ge(w_in_slot[blk % 4], 16 * (blk // 4 + 1))
                back = blk - 2
                if 0 <= back < CH_K:
                    pe.wait_ge(gate_out, back + 1)
                elif back == CH_K:
                    pe.wait_ge(raw_ready, 1)
                elif back == CH_V:
                    pe.wait_ge(v_copied, 1)
                elif back >= CH_Q:
                    pe.wait_ge(raw_ready, back - CH_Q + 2)
                w = wbuf[:, blk % 4, :, :]
                if blk == CH_V:
                    for n in range(NT):
                        for k in range(DK):
                            last = mm(ps[:, 2 + n // 4, (n % 4) * P:(n % 4 + 1) * P], wide[:, k, n * P:(n + 1) * P],
                                      w[:, k, :], start=k == 0, stop=k == DK - 1)
                else:
                    for k in range(DK):
                        if blk == 0:
                            pe.wait_ge(hn_ready, k + 1)
                        for hb in range(2):
                            last = mm(ps[:, 2 * (blk % 2) + hb, :], w[:, k, :], wide[:, k, hb * 512:(hb + 1) * 512],
                                      start=k == 0, stop=k == DK - 1)
                last.then_inc(proj_ready, 1)
                if blk == CH_V:
                    rotate(0)
                if blk > CH_Q:
                    rotate(blk - CH_Q)

            def scores(s):
                n, g = STEPS[s]
                if s >= 2:
                    pe.wait_ge(sc_free, s - 1)
                for j in range(GQ):
                    last = mm(ps[:, 2 * (s % 2) + j // 2, (j % 2) * 256:(j % 2 + 1) * 256],
                              qT[g * HD:(g + 1) * HD, j, n * P:(n + 1) * P], kT[g * HD:(g + 1) * HD, n * P:n * P + 2 * P],
                              start=True, stop=True)
                last.then_inc(sc_ready, 1)

            rotate(GQ)
            pe.wait_ge(rope_done, 1 + GQ)
            pe.wait_ge(pads_ready, 1)

            def turn_probs(s):
                pe.wait_ge(p_ready, s + 1)
                if s:
                    pe.wait_ge(pt_copied, s)
                for j in range(2 * GQ):
                    last = nc.tensor.transpose(ps[:, 4 + j // 4, (j % 4) * P:(j % 4 + 1) * P],
                                               sm[:, s % 3, j // 2, (j % 2) * P:(j % 2 + 1) * P], ident)
                last.then_inc(pt_ready, 1)

            def weigh(s):
                n, g = STEPS[s]
                pe.wait_ge(pt_copied, s + 1)
                if s >= 2:
                    pe.wait_ge(o_done, s - 1)
                for j in range(GQ):
                    for kb in range(2):
                        last = mm(ps[:, 6 + s % 2, j * HD:(j + 1) * HD], pT[:, 2 * j + kb, :],
                                  vv[:, n + kb, g * HD:(g + 1) * HD], start=kb == 0, stop=kb == 1)
                last.then_inc(o_ready, 1)

            scores(0)
            scores(1)
            for s in range(NS):
                turn_probs(s)
                if s + 2 < NS:
                    scores(s + 2)
                weigh(s)

            pe.wait_ge(sc_free, NS)
            pe.wait_ge(conv_dve, CC - 2)
            pe.wait_ge(conv_pool, 2)
            for c in range(CC):
                last = sum_rows(0, hnT[:, 4 + c, :], c, CC)
            last.then_inc(ln_sum, 1)
            for r, bank in ((0, 2), (1, 0)):
                for c in range(CC):
                    pe.wait_ge(ln_sq, r * CC + c + 1)
                    sum_rows(bank, tmp[:, c % 2, :], c, CC).then_inc(ln_used, 1)

            for n in range(NT):
                pe.wait_ge(ao_scaled, n + 1)
                if n >= 2:
                    pe.wait_ge(ao_mixed, n - 1)
                for m in range(4):
                    last = nc.tensor.transpose(ps[:, 4 + n % 2, m * P:(m + 1) * P], o_all[:, n, m * P:(m + 1) * P], ident)
                last.then_inc(ao_t, 1)

            def turn(n):
                pe.wait_ge(h_scaled, n + 1)
                if n >= 2:
                    pe.wait_ge(hnT_ready, n - 1)
                for m in range(DK):
                    last = nc.tensor.transpose(ps[:, 4 + 2 * (n % 2) + m // 4, (m % 4) * P:(m % 4 + 1) * P],
                                               tmp[:, n % 2, m * P:(m + 1) * P], ident)
                last.then_inc(h_t, 1)

            pe.wait_ge(wout_in, 16)
            pe.wait_ge(ln_y, 3 * CC)
            pe.wait_ge(ao_mixed, NT)
            for n in range(NT):
                if n >= 2:
                    pe.wait_ge(h_ready, n - 1)
                for hb in range(2):
                    for m in range(DK):
                        last = mm(ps[:, 2 * (n % 2) + hb, :], hnT[:, m, n * P:(n + 1) * P],
                                  wide[:, m, hb * 512:(hb + 1) * 512], start=m == 0, stop=m == DK - 1)
                last.then_inc(wo_ready, 1)
                if n:
                    turn(n - 1)
            turn(NT - 1)

            def key_scores(m):
                pe.wait_ge(q_copied, m + 1)
                if m >= 2:
                    pe.wait_ge(ks_free, m - 1)
                for n in range(HT):
                    last = mm(ps[:, 2 + m % 2, n * P:(n + 1) * P], qc[:, m % 2, n * P:(n + 1) * P], keys[:, m % HP, :],
                              start=True, stop=True)
                last.then_inc(ks_ready, 1)

            def query(m, k0, k1):
                if k0 == 0:
                    pe.wait_ge(wq_in_slot[m % 4], 16 * (m // 4 + 1))
                    if m >= 2:
                        pe.wait_ge(q_copied, m - 1)
                t0 = m // HP * HALF
                for k in range(k0, k1):
                    last = mm(ps[:, m % 2, :], wqbuf[:, m % 4, k, :], hnT[:, k, t0:t0 + HALF], start=k == 0, stop=k == DK - 1)
                if k1 == DK:
                    last.then_inc(q_ready, 1)

            pe.wait_ge(hnT_ready, NT)
            pe.wait_ge(h_ready, NT)
            pe.wait_ge(keys_in, 16)
            for m in range(ALONE):
                query(m, 0, DK)
                if m:
                    key_scores(m - 1)

            pe.sem_inc(gp_ready, ROWS_CREDIT)

            def turn_selected(i):
                pe.wait_ge(sel_ready, i + 1)
                for d in range(3):
                    last = nc.tensor.transpose(ps[:, 5, d * P:(d + 1) * P], sel3[:, d, :], ident)
                last.then_inc(selT_ps, 1)

            def tile(i, u, ahead=2, mixed=False):
                for b in range(BLOCKS):
                    if mixed:
                        n = i * BLOCKS + b
                        unit, part = ALONE + n // SPREAD, n % SPREAD
                        if unit < UNITS:
                            query(unit, -(-DK * part // SPREAD), -(-DK * (part + 1) // SPREAD))
                        if part == 0 and unit <= UNITS:
                            key_scores(unit - 1)
                    pe.wait_ge(hot_plain, i * BLOCKS + b + 1 + RAW)
                    pe.wait_ge(hot_scaled, i * BLOCKS + b + 1 + RAW)
                    for e in range(HQ):
                        pe.wait_ge(gp_free, (i * BLOCKS + b) * HQ + e + 1)
                        for q in range(4):
                            last = mm(ps[:, 6 + e, q * P:(q + 1) * P], hot[:, b % ROWS, 1, e * 4 + q, :],
                                      hot[:, b % ROWS, 0, e * 4 + q, :], start=True, stop=True)
                        last.then_inc(gp_ready, 1)
                    if ahead and b == TURN_AFTER:
                        turn_selected(i + 1)

            turn_selected(0)
            for i in range(MIXED_TILES):
                tile(i, i % 2, mixed=True)
            with pe.Fori(MIXED_TILES // 2, NT // 2 - 1) as j:
                for u in range(2):
                    tile(j * 2 + u, u)
            tile(NT - 2, 0, ahead=1)
            tile(NT - 1, 1, ahead=0)

            def group(half, g, first=False):
                G = half * NG + g
                for c in range(GC):
                    n = half * NKEY + g * GC + c
                    pe.wait_ge(ul_ready, n + 1)
                    pe.wait_ge(uh_ready, n + 1)
                    if not first or c >= 2:
                        pe.wait_ge(gelu_ready, n - 1)
                    for k in range(DK):
                        for w, xx in ((uh, xh), (uh, xl), (ul, xh)):
                            last = mm(ps[:, c % 2, :], w[:, c % 2, k, :], xx[:, k, :],
                                      start=k == 0 and w is uh and xx is xh, stop=k == DK - 1 and w is ul)
                    last.then_inc(hp_ready, 1)

                def second(k, cs):
                    tt, dh = k % HT, k // HT
                    for c in cs:
                        for w, v in ((wh, vh), (wh, vl), (wl, vh)):
                            last = mm(ps[:, 2 + k % 4, :], w[:, c, tt * P:(tt + 1) * P], v[:, c, dh * 512:(dh + 1) * 512],
                                      start=c == 0 and w is wh and v is vh, stop=c == GC - 1 and w is wl)
                    return last

                pe.wait_ge(wl_ready, half * NKEY + g * GC + GC - 1)
                for k in range(2):
                    if not first:
                        pe.wait_ge(op_free, G * 8 + k - 3)
                    second(k, range(GC - 1))
                pe.wait_ge(wl_ready, half * NKEY + g * GC + GC)
                for k in range(2):
                    second(k, [GC - 1]).then_inc(op_ready, 1)
                for k in range(2, 8):
                    if not first or k >= 4:
                        pe.wait_ge(op_free, G * 8 + k - 3)
                    second(k, range(GC)).then_inc(op_ready, 1)

            for half in range(2):
                pe.wait_ge(xl_ready, (half + 1) * DK)
                if half == 0:
                    group(0, 0, first=True)
                with pe.Fori(1 - half, NG) as g:
                    group(half, g)


_INS = ["x", "norm_mix_g", "w_in", "conv_w", "conv_b", "conv_ln_g", "conv_ln_b", "attn_sinks", "attn_out_g",
        "conv_out_g", "w_out", "norm_ffn_g", "peer_w_q", "peer_sub_keys", "peer_u", "peer_v", "final_norm_g"]


def constants():
    import numpy as np

    con = np.zeros((P, C_END), np.float32)
    con[:, C_ID:C_ID + P] = np.eye(P)
    con[:, C_ONE:C_ONE + P] = 1
    con[:, C_IOTA:C_IOTA + P] = np.arange(P)
    half = HD // 2
    for m in range(P):
        first = m % HD < half
        con[m + half if first else m - half, C_ROT + m] = -1 if first else 1
    rel = np.arange(P)[:, None] + P - np.arange(2 * P)[None, :]
    band = (rel >= 0) & (rel < P)
    con[:, C_MASK:C_MASK + 2 * P] = np.where(band, 0, NEG)
    con[:, C_MASK0:C_MASK0 + 2 * P] = np.where(band & (np.arange(2 * P)[None, :] >= P), 0, NEG)
    inv = (10000.0 ** (-np.arange(half) / half)).astype(np.float32)
    ang = np.arange(T, dtype=np.float32)[None, :] * inv[:, None]
    con[:, C_COS:C_COS + T] = np.tile(np.cos(ang.astype(np.float64)), (P // half, 1))
    con[:, C_SIN:C_SIN + T] = np.tile(np.sin(ang.astype(np.float64)), (P // half, 1))
    return con


def kernel(**inputs):
    import numpy as np
    import concourse.bacc as bacc
    from concourse.bass_utils import run_bass_kernel_spmd

    a = {k: np.asarray(inputs[k]) for k in _INS}

    def rows(m):
        return m.reshape(m.shape[0] // P, P, -1).transpose(1, 0, 2)

    def cols(v):
        return v.reshape(-1, P).T

    x = a["x"].reshape(T, D)
    w_in = a["w_in"][0]
    q_cols = np.arange(HEADS * HD).reshape(KVH, GQ, HD).transpose(1, 0, 2).reshape(GQ, P)
    blocks = []
    for c in range(CC):
        blocks += [np.arange(768 + c * P, 768 + (c + 1) * P), np.arange(1280 + c * P, 1280 + (c + 1) * P)]
    blocks += [np.arange(512, 640), np.arange(640, 768), *q_cols]
    w_blocks = np.stack([rows(w_in[:, b]) for b in blocks])
    w_q = np.stack([rows(b) for b in np.split(a["peer_w_q"][0], HP, axis=1)])
    keysT = a["peer_sub_keys"][0].reshape(HP, NKEY, P).transpose(2, 0, 1)
    uT = a["peer_u"][0].reshape(NKEY, P, DK, P).transpose(0, 3, 2, 1).reshape(NKEY, P, D)
    v_tab = a["peer_v"][0].reshape(NKEY, P, D)
    conv_w = a["conv_w"][0].T.reshape(CC, P, TAPS).transpose(1, 0, 2).reshape(P, CC * TAPS)
    params = np.concatenate(
        [cols(a["norm_mix_g"][0]), cols(a["norm_ffn_g"][0]), cols(a["attn_out_g"][0]), cols(a["conv_out_g"][0]),
         cols(a["conv_b"][0]), cols(a["conv_ln_g"][0]), cols(a["conv_ln_b"][0]),
         np.tile(a["attn_sinks"][0][None, :], (P, 1)), conv_w, np.full((P, 1), EPS, np.float32)], axis=1)
    data = {"x": x, "xT": rows(np.ascontiguousarray(x.T)), "w_in": w_blocks, "w_out": rows(a["w_out"][0]), "w_q": w_q,
            "keysT": keysT, "uT": uT, "v_tab": v_tab, "consts": constants(), "params": params,
            "final_g": a["final_norm_g"]}

    nc = bacc.Bacc("TRN2", target_bir_lowering=False, num_devices=1)
    arrays, args = {}, []
    for name, v in data.items():
        arrays[f"in_{name}"] = np.ascontiguousarray(v)
        args.append(nc.dram_tensor(f"in_{name}", v.shape, mybir.dt.from_np(v.dtype), kind="ExternalInput").ap())
    args.append(nc.dram_tensor("out_y", (T, D), F32, kind="ExternalOutput").ap())
    decoder_block(nc, *args)
    r = run_bass_kernel_spmd(nc, [arrays], core_ids=[0])
    return r.results[0]["out_y"].reshape(1, T, D)
```

```python
from contextlib import ExitStack

import concourse.bass as bass
from concourse import mybir

P = 128
D = 1024
T = 1024
DK = D // P
NT = T // P
HEADS, KVH, HD = 8, 2, 64
GQ = HEADS // KVH
CONV = 512
CC = CONV // P
TAPS = 31
PH = 8
HP = 2 * PH
NKEY = 128
TOPK = 16
EPS = 1e-6
NEG = -1e30
LOWEST = -3.0e38
HALF = T // 2
HT = HALF // P
SUB = 32
HOT = 8
HQ = HOT // 4
BLOCKS = P // HOT
RAW = 4
ROWS = 2
ROWS_CREDIT = ROWS * HQ
BANKS = 2
WIDE = 4
NCAND = WIDE * TOPK + (TOPK - WIDE) * WIDE
UNITS = 2 * HP
ALONE = 20
SPREAD = 3
MIXED_TILES = 4
STEPS_PICK = 14
EARLY_STEPS = 7
LATE_STEPS = {0: 7, 1: 8, 2: 9, 4: 10, 5: 11, 6: 12, 7: 13}
SUMS_AFTER = 5
TURN_AFTER = 9
GC = 4
NG = NKEY // GC

CH_GATE = (0, 2, 10, 12)
CH_K, CH_V, CH_Q = 4, 5, 6
NCH = 14
NCH_ALONE = 12
LAST_C = CC - 1
CONV_STEP = 9
CONV_TAPS = 5

C_ID, C_ONE, C_IOTA, C_ROT, C_MASK0, C_MASK, C_COS, C_SIN = 0, 128, 256, 384, 512, 768, 1024, 2048
C_END = 3072
G_MIX, G_FFN, G_ATT, G_CONV, B_CONV, LN_G, LN_B, SINK, CW = 0, 8, 16, 20, 24, 28, 32, 36, 44
G_EPS = CW + CC * TAPS
G_END = G_EPS + 1

F32 = mybir.dt.float32
F32R = mybir.dt.float32r
U32 = mybir.dt.uint32
BF16 = mybir.dt.bfloat16
ALU = mybir.AluOpType
ACT = mybir.ActivationFunctionType
AX = mybir.AxisListType


def decoder_block(nc, x, xT, w_in, w_out, w_q, keysT, uT, v_tab, consts, params, final_g, out):
    gates = nc.dram_tensor("gates", (2, NG, P, HALF // SUB, GC, SUB), F32, kind="Internal").ap()

    ctx = ExitStack()
    early = ExitStack()
    late = ExitStack()

    def sb(name, shape, dt=F32, where=ctx):
        return where.enter_context(nc.sbuf_tensor(name, shape, dt))

    def sem(name):
        return ctx.enter_context(nc.semaphore(name))

    with ctx:
        acc = sb("acc", [P, NT, D])
        hnT = sb("hnT", [P, DK, T])
        con = sb("con", [P, C_COS])
        par = sb("par", [P, G_END])
        small = sb("small", [P, 64])
        ident = con[:, C_ID:C_ID + P]
        ones = con[:, C_ONE:C_ONE + P]
        iota = con[:, C_IOTA:C_IOTA + P]

        rope = sb("rope", [P, 2, T], where=early)
        wide = sb("wide", [P, DK, T], where=early)
        wbuf = sb("wbuf", [P, 4, DK, P], where=early)
        ubuf = sb("ubuf", [P, CC, T + TAPS - 1], where=early)
        tmp = sb("tmp", [P, 2, T], where=early)
        tmp2 = sb("tmp2", [P, T], where=early)
        rb = sb("rb", [P, T], where=early)
        qT = sb("qT", [P, GQ, T], where=early)
        kT = sb("kT", [P, P + T], where=early)
        vv = sb("vv", [P, NT + 1, P], where=early)
        sm = sb("sm", [P, 3, GQ, 2 * P], where=early)
        pT = sb("pT", [P, 2 * GQ, P], where=early)
        att = sb("att", [P, 4, 6, GQ], where=early)
        tap = sb("tap", [P, 2, T], where=early)
        early.close()
        o_all = acc[:, HT:NT, :].rearrange("p n (e d) -> p (n e) d", e=2)

        mid = ExitStack()
        s16 = sb("s16", [P, NT, HP, TOPK], where=mid)
        i16 = sb("i16", [P, HT, HP, TOPK], U32, where=mid)
        i16p = sb("i16p", [P, NT, HP, TOPK, 2], BF16, where=mid)
        keys = sb("keys", [P, HP, NKEY], where=mid)
        pick = ExitStack()
        picks = sb("picks", [P, 2, PH, TOPK // 2, TOPK, 2], BF16, where=pick)
        cand = sb("cand", [P, PH, NCAND], where=pick)
        cand2 = sb("cand2", [P, PH, NCAND], where=pick)
        wqbuf = sb("wqbuf", [P, 4, DK, P], where=pick)
        qc = sb("qc", [P, 2, HALF], where=pick)
        swork = sb("swork", [P, HT, NKEY], where=pick)
        best = sb("best", [P, PH, TOPK], where=pick)
        bpos = sb("bpos", [P, PH * TOPK], U32, where=pick)
        bdig = sb("bdig", [P, 5, PH * TOPK], U32, where=pick)
        bdigf = bdig[:, :, :].bitcast(F32)
        ranks = sb("ranks", [P, 2, PH * TOPK], BF16, where=pick)
        sel3 = sb("sel3", [P, 3, P], where=pick)
        selI = sb("selI", [P, 2, BLOCKS, 2, HOT], BF16, where=pick)
        selG = sb("selG", [P, 2, P], where=pick)
        iota2 = sb("iota2", [P, NKEY, 2], BF16, where=pick)
        marks = sb("marks", [P, RAW, 2, HOT // 2, NKEY, 2], BF16, where=pick)
        split = ExitStack()
        wqh = sb("wqh", [P, 2, DK, P], F32R, where=split)
        wql = sb("wql", [P, 2, DK, P], F32R, where=split)
        hnh = sb("hnh", [P, DK, HALF], F32R, where=split)
        hnl = sb("hnl", [P, DK, HALF], F32R, where=split)
        split.close()
        hot = sb("hot", [P, ROWS, 2, HOT, P], where=pick)
        gbuf = sb("gbuf", [P, 2, NKEY, SUB], where=pick)
        den = sb("den", [P, 2, PH], where=pick)
        pick.close()
        mid.close()

        xh = sb("xh", [P, DK, HALF], F32R, where=late)
        xl = sb("xl", [P, DK, HALF], F32R, where=late)
        u_raw = sb("u_raw", [P, 2, D], where=late)
        uh = sb("uh", [P, 2, DK, P], F32R, where=late)
        ul = sb("ul", [P, 2, DK, P], F32R, where=late)
        v_raw = sb("v_raw", [P, GC, D], where=late)
        vh = sb("vh", [P, GC, D], F32R, where=late)
        vl = sb("vl", [P, GC, D], F32R, where=late)
        gt = sb("gt", [P, HALF // SUB, GC, SUB], where=late)
        hg = sb("hg", [P, 2, HALF], where=late)
        wh = sb("wh", [P, GC, HALF], F32R, where=late)
        wl = sb("wl", [P, GC, HALF], F32R, where=late)
        fg = sb("fg", [P, D], where=late)
        late.close()

        ps = ctx.enter_context(nc.psum_tensor("ps", [P, 8, 512], F32))

        def candidate_sums(i, h0=0, h1=PH):
            st = s16[:, bass.ds(i, 1), :, :].rearrange("p o (h s) k -> p (o h) s k", s=2)
            return [(cand[:, h0:h1, a0 * TOPK:a0 * TOPK + na * nb].rearrange("p h (a b) -> p h a b", a=na),
                     st[:, h0:h1, 0, a0:a0 + na].unsqueeze(3).to_broadcast([P, h1 - h0, na, nb]),
                     st[:, h0:h1, 1, 0:nb].unsqueeze(2).to_broadcast([P, h1 - h0, na, nb]))
                    for a0, na, nb in ((0, WIDE, TOPK), (WIDE, TOPK - WIDE, WIDE))]

        def bank2(b):
            return ps[:, b:b + 2, :].rearrange("p b n -> p (b n)")

        consts_in, rope_in, params_in = sem("consts_in"), sem("rope_in"), sem("params_in")
        xT_in = [sem(f"xT_in{k}") for k in range(DK)]
        x_in = [sem("x_in0"), sem("x_in1")]
        w_in_slot = [sem(f"w_in_slot{k}") for k in range(4)]
        wq_in_slot = [sem(f"wq_in_slot{k}") for k in range(4)]
        wout_in, keys_in = sem("wout_in"), sem("keys_in")

        def sems(names):
            return [sem(n) for n in names.split()]

        pads_ready, sq_ready, sq_used, rms_root, hn_ready = sems("pads_ready sq_ready sq_used rms_root hn_ready")
        proj_ready = sem("proj_ready")
        raw_ready, rot_ready, rope_done, v_copied = sems("raw_ready rot_ready rope_done v_copied")
        gate_out, conv_dve, conv_pool, part_ready, part_out = sems("gate_out conv_dve conv_pool part_ready part_out")
        ln_sum, ln_stat, ln_y, ln_sq, ln_used = sems("ln_sum ln_stat ln_y ln_sq ln_used")
        sc_ready, sm_ready, sc_free, p_ready, pt_ready, pt_copied, o_ready, o_done = sems(
            "sc_ready sm_ready sc_free p_ready pt_ready pt_copied o_ready o_done")
        ao_root, ao_rec, ao_scaled, ao_t, ao_mixed, at_ready, at_added = sems(
            "ao_root ao_rec ao_scaled ao_t ao_mixed at_ready at_added")
        wo_ready, h_ready, h_root, h_rec, h_scaled, h_t, hnT_ready = sems(
            "wo_ready h_ready h_root h_rec h_scaled h_t hnT_ready")
        q_ready, q_copied, ks_ready, ks_free, hnh_ready, hnl_ready, wqh_ready, wql_ready = sems(
            "q_ready q_copied ks_ready ks_free hnh_ready hnl_ready wqh_ready wql_ready")
        best_ready, exp_ready, sums_ready, sel_ready, selT_ps, selT_ready = sems(
            "best_ready exp_ready sums_ready sel_ready selT_ps selT_ready")
        hot_eq, hot_plain, hot_scaled, gp_ready, gp_free = sems("hot_eq hot_plain hot_scaled gp_ready gp_free")
        gates_out = [sem("gates_out0"), sem("gates_out1")]
        xh_ready, xl_ready = sem("xh_ready"), sem("xl_ready")
        u_in = [sem(f"u_in{k}") for k in range(2)]
        v_in = [sem(f"v_in{k}") for k in range(GC)]
        g_in = sem("g_in")
        uh_ready, ul_ready, vh_ready, vl_ready = sems("uh_ready ul_ready vh_ready vl_ready")
        hp_ready, gelu_ready, w_ready, wh_ready, wl_ready = sems("hp_ready gelu_ready w_ready wh_ready wl_ready")
        op_ready, op_free = sems("op_ready op_free")
        f_root, f_ready, fg_in = sems("f_root f_ready fg_in")
        f_out = sem("f_out")

        block = ctx.enter_context(nc.Block())
        STEPS = [(n, g) for n in range(NT) for g in range(KVH)]
        NS = len(STEPS)
        PART_STEPS = 9

        def out_bank(s):
            return 7 if s >= PART_STEPS and s % 2 else 6

        @block.sync
        def _(sp):
            sp.dma_start(con[:, :], consts[:, 0:C_COS]).then_inc(consts_in, 16)
            sp.dma_start(par[:, :], params).then_inc(params_in, 16)
            for k in range(DK):
                sp.dma_start(wide[:, k, :], xT[:, k, :]).then_inc(xT_in[k], 16)
            for c in range(4):
                sp.dma_start(wbuf[:, c, :, :], w_in[c]).then_inc(w_in_slot[c], 16)
            sp.dma_start(rope[:, :, :], consts[:, C_COS:C_END].rearrange("p (s t) -> p s t", s=2)).then_inc(rope_in, 16)
            for c in range(4, NCH):
                sp.wait_ge(proj_ready, c - 3)
                sp.dma_start(wbuf[:, c % 4, :, :], w_in[c]).then_inc(w_in_slot[c % 4], 16)
            sp.dma_start(acc[:, 0:HT, :], x[0:HALF, :].rearrange("(n p) d -> p n d", p=P)).then_inc(x_in[0], 16)
            sp.wait_ge(part_ready, 4)
            sp.dma_start(wide[:, :, :], w_out).then_inc(wout_in, 16)
            sp.wait_ge(ao_t, NT)
            sp.dma_start(acc[:, HT:NT, :], x[HALF:T, :].rearrange("(n p) d -> p n d", p=P)).then_inc(x_in[1], 16)

            def load_wq(m):
                if 4 <= m < HP + 4:
                    sp.wait_ge(wql_ready, m - 3)
                elif m >= 4:
                    sp.wait_ge(q_ready, m - 3)
                sp.dma_start(wqbuf[:, m % 4, :, :], w_q[m % HP]).then_inc(wq_in_slot[m % 4], 16)

            def write_gates(half, m, s):
                sp.wait_ge(gp_free, (half * (HALF // SUB) + m + 1) * (SUB // 4) + BANKS)
                sp.dma_start(gates[half, :, :, bass.ds(m, 1), :, :].rearrange("g p o c t -> p g (o c t)"),
                             gbuf[:, s, :, :].rearrange("p (g c) t -> p g (c t)", c=GC)).then_inc(gates_out[s], 16)

            for m in range(4):
                load_wq(m)
            sp.wait_ge(wo_ready, NT)
            sp.dma_start(keys[:, :, :], keysT).then_inc(keys_in, 16)
            for m in range(4, ALONE + 4):
                load_wq(m)
            for n in range(MIXED_TILES * BLOCKS):
                unit = ALONE + n // SPREAD
                if n % SPREAD == SPREAD - 1 and unit + 4 < UNITS:
                    load_wq(unit + 4)
                if n % (SUB // HOT) == SUB // HOT - 1:
                    write_gates(0, n * HOT // SUB, n * HOT // SUB % 2)
            with sp.Fori(0, HALF // SUB // 2 - 2) as i:
                for s in range(2):
                    write_gates(1, i * 2 + s, s)
            sp.wait_ge(sel_ready, NT)
            for c in range(2):
                sp.dma_start(u_raw[:, c, :], uT[c]).then_inc(u_in[c], 16)
            for m in range(HALF // SUB - 4, HALF // SUB):
                write_gates(1, m, m % 2)
            for b in range(2):
                sp.wait_ge(gates_out[b], 16 * (T // SUB // 2))

            def load_gates(half, g):
                sp.dma_start(gt[:, :, :, :], gates[half, g]).then_inc(g_in, 16)

            def load_group(half, g, first=False):
                for c in range(GC):
                    n = half * NKEY + g * GC + c
                    if not first or c >= 2:
                        sp.wait_ge(uh_ready, n - 1)
                        sp.wait_ge(ul_ready, n - 1)
                        sp.dma_start(u_raw[:, c % 2, :], uT[g * GC + c]).then_inc(u_in[c % 2], 16)
                    if not first:
                        sp.wait_ge(vh_ready, n - GC + 1)
                        sp.wait_ge(vl_ready, n - GC + 1)
                    sp.dma_start(v_raw[:, c, :], v_tab[g * GC + c]).then_inc(v_in[c], 16)
                    if first and c == 0:
                        load_gates(half, g)
                if not first:
                    sp.wait_ge(w_ready, half * NKEY + g * GC)
                    load_gates(half, g)

            load_group(0, 0, first=True)
            sp.dma_start(fg[:, :], final_g.partition_broadcast(P)).then_inc(fg_in, 16)
            with sp.Fori(1, NG) as g:
                load_group(0, g)
            with sp.Fori(0, NG) as g:
                load_group(1, g)
            for n in range(NT):
                sp.wait_ge(f_ready, n + 1)
                sp.dma_start(out[n * P:(n + 1) * P, :], acc[:, n, :]).then_inc(f_out, 16)
            sp.wait_ge(f_out, 16 * NT)

        @block.gpsimd
        def _(pool):
            nc.gpsimd.memset(ubuf[:, :, 0:TAPS - 1], 0.0)
            nc.gpsimd.memset(kT[:, 0:P], 0.0)
            nc.gpsimd.memset(vv[:, 0, :], 0.0).then_inc(pads_ready, 1)
            pool.wait_ge(pads_ready, 1)
            for c in (0, 2):
                u, y = ubuf[:, c, TAPS - 1:], hnT[:, 4 + c, :]
                pool.wait_ge(gate_out, 2 * c + 2)
                nc.gpsimd.tensor_tensor(u, u, y, ALU.mult)
                pool.drain()
                nc.gpsimd.tensor_scalar(y, ubuf[:, c, 0:T], par[:, CW + c * TAPS:CW + c * TAPS + 1],
                                        par[:, B_CONV + c:B_CONV + c + 1], ALU.mult, ALU.add)
                for k in range(1, TAPS):
                    nc.gpsimd.tensor_scalar(tap[:, k % 2, :], ubuf[:, c, k:k + T],
                                            par[:, CW + c * TAPS + k:CW + c * TAPS + k + 1], 0.0, ALU.mult, ALU.add)
                    pool.drain()
                    nc.gpsimd.tensor_tensor(y, y, tap[:, k % 2, :], ALU.add)
                pool.drain()
                pool.sem_inc(conv_pool, 1)

            for m in range(HP):
                pool.wait_ge(wqh_ready, m + 1)
                nc.gpsimd.tensor_tensor(wql[:, m % 2, :, :], wqbuf[:, m % 4, :, :], wqh[:, m % 2, :, :].bitcast(F32),
                                        ALU.subtract).then_inc(wql_ready, 1)

            pool.sem_inc(hot_scaled, RAW)

            def tile(i, u, ahead=2, mixed=False):
                for b in range(BLOCKS):
                    n = i * BLOCKS + b
                    pool.wait_ge(hot_eq, n + 1)
                    pool.wait_ge(gp_ready, (n + 1) * HQ)
                    gate = selG[:, u, b * HOT:(b + 1) * HOT].rearrange("p (c e) -> p c e", e=2)
                    nc.gpsimd.tensor_tensor(hot[:, b % ROWS, 1, :, :].rearrange("p (c e) k -> p c e k", e=2),
                                            marks[:, b % RAW, 1, :, :, :].rearrange("p c k e -> p c e k"),
                                            gate.unsqueeze(3).to_broadcast([P, HOT // 2, 2, NKEY]),
                                            ALU.mult).then_inc(hot_scaled, 1)
                    if ahead > 1 and b == SUMS_AFTER and not (mixed and i + 2 == HT):
                        for out, in0, in1 in candidate_sums(i + 2):
                            last = nc.gpsimd.tensor_tensor(out, in0, in1, ALU.add)
                        last.then_inc(sums_ready, 1)

            for i in range(MIXED_TILES):
                tile(i, i % 2, mixed=True)
            with pool.Fori(MIXED_TILES // 2, NT // 2 - 1) as j:
                for u in range(2):
                    tile(j * 2 + u, u)
            tile(NT - 2, 0, ahead=1)
            tile(NT - 1, 1, ahead=0)

        @block.scalar
        def _(act):
            for k in range(DK):
                act.wait_ge(xT_in[k], 16)
                if k >= 2:
                    act.wait_ge(sq_used, k - 1)
                nc.scalar.activation(tmp[:, k % 2, :], wide[:, k, :], ACT.Square).then_inc(sq_ready, 1)
            act.wait_ge(sq_used, DK)
            act.wait_ge(params_in, 16)
            nc.scalar.activation(rb[:, :], bank2(0), ACT.Sqrt, bias=par[:, G_EPS:G_END], scale=1.0 / D).then_inc(rms_root, 1)

            def copy_raw(r, blk):
                act.wait_ge(proj_ready, blk + 1)
                if r >= 2:
                    act.wait_ge(rope_done, r - 1)
                nc.scalar.copy(tmp[:, r % 2, :], bank2(2 * (blk % 2))).then_inc(raw_ready, 1)

            def gated(c):
                act.wait_ge(proj_ready, CH_GATE[c] + 1)
                nc.scalar.copy(ubuf[:, c, TAPS - 1:], bank2(0)).then_inc(gate_out, 1)
                act.wait_ge(proj_ready, CH_GATE[c] + 2)
                nc.scalar.activation(hnT[:, 4 + c, :], bank2(2), ACT.Sigmoid).then_inc(gate_out, 1)

            gated(0)
            gated(1)
            copy_raw(0, CH_K)
            act.wait_ge(proj_ready, CH_V + 1)
            nc.scalar.copy(vv[:, 1:NT + 1, :].rearrange("p n d -> p (n d)"), bank2(2 * (CH_V % 2))).then_inc(v_copied, 1)
            for j in range(GQ):
                copy_raw(1 + j, CH_Q + j)
            gated(2)

            def copy_part(j):
                act.wait_ge(part_ready, j + 1)
                t0 = j % 2 * HALF
                dst = ubuf[:, LAST_C, TAPS - 1 + t0:TAPS - 1 + t0 + HALF] if j < 2 else hnT[:, 4 + LAST_C, t0:t0 + HALF]
                nc.scalar.copy(dst, ps[:, 7, :]).then_inc(part_out, 1)
                if j == 3:
                    act.drain()
                    y = hnT[:, 4 + LAST_C, :]
                    nc.scalar.activation(y, y, ACT.Sigmoid).then_inc(gate_out, 2)

            def probs(s):
                act.wait_ge(sm_ready, s + 1)
                for j in range(GQ):
                    nc.scalar.activation(sm[:, s % 3, j, :], sm[:, s % 3, j, :], ACT.Exp, bias=att[:, s % 4, 1, j:j + 1],
                                         accum_out=att[:, s % 4, 3, j:j + 1])
                nc.scalar.activation(att[:, s % 4, 4, :], att[:, s % 4, 2, :], ACT.Exp).then_inc(p_ready, 1)

            def out_squares(n):
                act.wait_ge(o_done, 2 * n + 2)
                nc.scalar.activation(tmp2[:, 0:512], o_all[:, n, :], ACT.Square, accum_out=small[:, n:n + 1])
                act.drain()

            for s in range(NS + 1):
                if s < NS:
                    probs(s)
                if s:
                    act.wait_ge(pt_ready, s)
                    if s >= 2:
                        act.wait_ge(o_ready, s - 1)
                    nc.scalar.copy(pT[:, :, :].rearrange("p j q -> p (j q)"), bank2(4)).then_inc(pt_copied, 1)
                if s % 2 == 0 and 2 <= s <= 8:
                    copy_part(s // 2 - 1)
                if s % 2 and s >= 5:
                    out_squares((s - 5) // 2)

            out_squares(NT - 2)
            out_squares(NT - 1)
            nc.scalar.activation(small[:, 8:16], small[:, 0:8], ACT.Sqrt, bias=par[:, G_EPS:G_END],
                                 scale=1.0 / 512).then_inc(ao_root, 1)

            def scale_out(n):
                nc.scalar.mul(o_all[:, n, :], o_all[:, n, :], small[:, 16 + n:17 + n]).then_inc(ao_scaled, 1)

            act.wait_ge(ao_rec, 1)
            for n in range(4):
                scale_out(n)
            act.wait_ge(ln_sum, 1)
            nc.scalar.mul(rb[:, :], bank2(0), 1.0 / CONV).then_inc(ln_stat, 1)
            for n in range(4, NT):
                scale_out(n)

            def squares(c, k, waits):
                act.wait_ge(ln_y, waits)
                if k >= 2:
                    act.wait_ge(ln_used, k - 1)
                nc.scalar.activation(tmp[:, k % 2, :], hnT[:, 4 + c, :], ACT.Square).then_inc(ln_sq, 1)

            for c in range(CC):
                squares(c, c, c + 1)
            act.wait_ge(ln_used, CC)
            nc.scalar.activation(rb[:, :], bank2(0), ACT.Sqrt, bias=par[:, G_EPS:G_END], scale=1.0 / CONV).then_inc(ln_stat, 1)
            for c in range(CC):
                act.wait_ge(ln_y, CC + c + 1)
                y = hnT[:, 4 + c, :]
                nc.scalar.activation(y, y, ACT.Silu, bias=par[:, LN_B + c:LN_B + c + 1], scale=par[:, LN_G + c:LN_G + c + 1])
                act.drain()
                if CC + c >= 2:
                    act.wait_ge(ln_used, CC + c - 1)
                nc.scalar.activation(tmp[:, c % 2, :], y, ACT.Square).then_inc(ln_sq, 1)
            act.wait_ge(ln_used, 2 * CC)
            nc.scalar.activation(rb[:, :], bank2(0), ACT.Sqrt, bias=par[:, G_EPS:G_END], scale=1.0 / CONV).then_inc(ln_stat, 1)

            def root(n):
                act.wait_ge(h_ready, n + 1)
                nc.scalar.activation(tmp2[:, :], acc[:, n, :], ACT.Square, accum_out=small[:, 24 + n:25 + n])
                act.drain()
                nc.scalar.activation(small[:, 32 + n:33 + n], small[:, 24 + n:25 + n], ACT.Sqrt,
                                     bias=par[:, G_EPS:G_END], scale=1.0 / D).then_inc(h_root, 1)

            def split_wq(m):
                act.wait_ge(wq_in_slot[m % 4], 16 * (m // 4 + 1))
                if m >= 2:
                    act.wait_ge(q_ready, m - 1)
                nc.scalar.copy(wqh[:, m % 2, :, :], wqbuf[:, m % 4, :, :]).then_inc(wqh_ready, 1)

            act.wait_ge(ln_y, 3 * CC)
            split_wq(0)
            split_wq(1)
            for n in range(NT):
                root(n)
                act.wait_ge(h_rec, n + 1)
                if n >= 2:
                    act.wait_ge(h_t, n - 1)
                nc.scalar.mul(tmp[:, n % 2, :], acc[:, n, :], small[:, 40 + n:41 + n]).then_inc(h_scaled, 1)
                if n in (HT + 1, HT + 2):
                    act.wait_ge(hnT_ready, HT)
                    for k in range((n - HT - 1) * 4, (n - HT) * 4):
                        nc.scalar.copy(hnh[:, k, :], hnT[:, k, 0:HALF]).then_inc(hnh_ready, 1)

            def copy_query(m):
                act.wait_ge(q_ready, m + 1)
                if m >= 2:
                    act.wait_ge(ks_ready, m - 1)
                nc.scalar.copy(qc[:, m % 2, :], ps[:, m % 2, :]).then_inc(q_copied, 1)

            def high_x(half, k):
                nc.scalar.copy(xh[:, k, :], hnT[:, k, half * HALF:(half + 1) * HALF]).then_inc(xh_ready, 1)

            def split_u(half, g, c):
                act.wait_ge(u_in[c % 2], 16 * (half * (NKEY // 2) + g * (GC // 2) + c // 2 + 1))
                nc.scalar.copy(uh[:, c % 2, :, :].rearrange("p k e -> p (k e)"), u_raw[:, c % 2, :]).then_inc(uh_ready, 1)

            def exps(i):
                act.wait_ge(best_ready, i + 1)
                nc.scalar.activation(best[:, :, :], best[:, :, :], ACT.Exp).then_inc(exp_ready, 1)

            def selected(i, u):
                act.wait_ge(selT_ps, i + 1)
                nc.scalar.copy(selI[:, u, :, :, :], ps[:, 5, 0:2 * P].rearrange("p (d b t) -> p b d t", d=2, b=BLOCKS))
                nc.scalar.copy(selG[:, u, :], ps[:, 5, 2 * P:3 * P]).then_inc(selT_ready, 1)

            def plain(i, b):
                n = i * BLOCKS + b
                act.wait_ge(hot_eq, n + 1)
                act.wait_ge(gp_ready, (n + 1) * HQ)
                nc.scalar.copy(hot[:, b % ROWS, 0, :, :].rearrange("p (c e) k -> p c e k", e=2),
                               marks[:, b % RAW, 0, :, :, :].rearrange("p c k e -> p c e k")).then_inc(hot_plain, 1)

            def gather(i, b):
                m = b * HOT // SUB
                s = m % 2
                if b * HOT % SUB == 0:
                    act.wait_ge(gates_out[s], (i * (P // SUB // 2) + m // 2) * 16)
                for e in range(HQ):
                    t0 = b * HOT % SUB + e * 4
                    act.wait_ge(gp_ready, (i * BLOCKS + b) * HQ + e + 1 + ROWS_CREDIT)
                    nc.scalar.copy(gbuf[:, s, :, t0:t0 + 4].rearrange("p i t -> p t i"),
                                   ps[:, 6 + e, :].rearrange("p (t i) -> p t i", t=4)).then_inc(gp_free, 1)

            def tile(i, u, ahead=2, mixed=False):
                for b in range(BLOCKS):
                    if mixed:
                        unit = ALONE + (i * BLOCKS + b) // SPREAD
                        if (i * BLOCKS + b) % SPREAD == 0 and ALONE < unit <= UNITS:
                            copy_query(unit - 1)
                    plain(i, b)
                    if b:
                        gather(i, b - 1)
                    if ahead and b == 1:
                        exps(i + 1)
                    if ahead and b == TURN_AFTER + 1:
                        selected(i + 1, 1 - u)
                    if ahead == 0:
                        if b == 1:
                            act.wait_ge(sel_ready, NT)
                        if 1 <= b <= DK:
                            high_x(0, b - 1)
                        elif b in (DK + 1, DK + 2):
                            split_u(0, 0, b - DK - 1)
                gather(i, BLOCKS - 1)

            for m in range(ALONE):
                copy_query(m)
                if m + 2 < HP:
                    split_wq(m + 2)
                if m == HP + 1:
                    act.sem_inc(gp_free, BANKS)
                    act.sem_inc(hot_plain, RAW)
                    exps(0)
            selected(0, 0)
            for i in range(MIXED_TILES):
                tile(i, i % 2, mixed=True)
            with act.Fori(MIXED_TILES // 2, NT // 2 - 1) as j:
                for u in range(2):
                    tile(j * 2 + u, u)
            tile(NT - 2, 0, ahead=1)
            tile(NT - 1, 1, ahead=0)

            for b in range(2):
                act.wait_ge(gates_out[b], 16 * (T // SUB // 2))

            def group(half, g, first=False, last=False):
                n0 = half * NKEY + g * GC
                if not first:
                    act.wait_ge(op_ready, (half * NG + g) * 8)
                for c in range(GC):
                    n = n0 + c
                    act.wait_ge(v_in[c], 16 * (half * NG + g + 1))
                    nc.scalar.copy(vh[:, c, :], v_raw[:, c, :]).then_inc(vh_ready, 1)
                    act.wait_ge(hp_ready, n + 1)
                    if not first or c >= 2:
                        act.wait_ge(wl_ready, n - 1)
                    nc.scalar.activation(hg[:, c % 2, :], ps[:, c % 2, :], ACT.Gelu).then_inc(gelu_ready, 1)
                    act.wait_ge(w_ready, n + 1)
                    nc.scalar.copy(wh[:, c, :], hg[:, c % 2, :]).then_inc(wh_ready, 1)
                    if c < 2:
                        split_u(half, g, c + 2)
                    elif not last:
                        split_u(half, g + 1, c - 2)

            def final_squares(n):
                nc.scalar.activation(bank2(6), acc[:, n, :], ACT.Square, accum_out=small[:, n:n + 1])
                act.drain()

            def final_root(n0, n1):
                nc.scalar.activation(small[:, 8 + n0:8 + n1], small[:, n0:n1], ACT.Sqrt, bias=par[:, G_EPS:G_END],
                                     scale=1.0 / D).then_inc(f_root, 1)

            for half in range(2):
                if half:
                    act.wait_ge(hp_ready, NKEY)
                    for k in range(DK):
                        high_x(half, k)
                    split_u(half, 0, 0)
                    split_u(half, 0, 1)
                if half == 0:
                    group(0, 0, first=True)
                with act.Fori(1 - half, NG - 1) as g:
                    group(half, g)
                if half:
                    for n in range(HT):
                        final_squares(n)
                    final_root(0, HT)
                group(half, NG - 1, last=True)

            for t in range(HT):
                act.wait_ge(op_free, (2 * NG - 1) * 8 + HT + t + 1)
                final_squares(HT + t)
                final_root(HT + t, HT + t + 1)

        @block.vector
        def _(dve):
            dve.wait_ge(rms_root, 1)
            nc.vector.reciprocal(rb[:, :], rb[:, :])
            dve.drain()
            for k in range(DK):
                nc.vector.scalar_tensor_tensor(out=wide[:, k, :], in0=wide[:, k, :], scalar=par[:, G_MIX + k:G_MIX + k + 1],
                                               in1=rb[:, :], op0=ALU.mult, op1=ALU.mult).then_inc(hn_ready, 1)

            dve.wait_ge(pads_ready, 1)
            def gate_values(c):
                u = ubuf[:, c, TAPS - 1:]
                dve.wait_ge(gate_out, 2 * c + 2)
                nc.vector.tensor_tensor(u, u, hnT[:, 4 + c, :], ALU.mult)

            def first_tap(c):
                dve.drain()
                nc.vector.tensor_scalar(hnT[:, 4 + c, :], ubuf[:, c, 0:T], par[:, CW + c * TAPS:CW + c * TAPS + 1],
                                        par[:, B_CONV + c:B_CONV + c + 1], ALU.mult, ALU.add)

            def add_tap(c, k):
                y = hnT[:, 4 + c, :]
                dve.drain()
                nc.vector.scalar_tensor_tensor(out=y, in0=ubuf[:, c, bass.ds(k, T)],
                                               scalar=par[:, bass.ds(k + CW + c * TAPS, 1)], in1=y,
                                               op0=ALU.mult, op1=ALU.add)

            gate_values(1)
            first_tap(1)
            with dve.Fori(0, (TAPS - 1) // 5) as r:
                for j in range(5):
                    add_tap(1, r * 5 + j + 1)
            dve.drain()
            dve.sem_inc(conv_dve, 1)

            dve.wait_ge(rope_in, 16)
            for r in range(1 + GQ):
                dst = kT[:, P:P + T] if r == 0 else qT[:, r - 1, :]
                dve.wait_ge(raw_ready, r + 1)
                nc.vector.tensor_tensor(dst, tmp[:, r % 2, :], rope[:, 0, :], ALU.mult)
                dve.wait_ge(rot_ready, r + 1)
                nc.vector.tensor_tensor(tmp2[:, :], bank2(4), rope[:, 1, :], ALU.mult)
                dve.drain()
                nc.vector.tensor_tensor(dst, dst, tmp2[:, :], ALU.add).then_inc(rope_done, 1)

            def soft(s):
                n, g = STEPS[s]
                b, m = s % 4, s % 3
                mask = con[:, C_MASK0:C_MASK0 + 2 * P] if n == 0 else con[:, C_MASK:C_MASK + 2 * P]
                sink = par[:, SINK + g * GQ:SINK + (g + 1) * GQ]
                dve.wait_ge(sc_ready, s + 1)
                if s >= 3:
                    dve.wait_ge(pt_ready, s - 2)
                nc.vector.scalar_tensor_tensor(
                    out=sm[:, m, :, :], in0=bank2(2 * (s % 2)).rearrange("p (j k) -> p j k", j=GQ), scalar=float(HD) ** -0.5,
                    in1=mask.unsqueeze(1).to_broadcast([P, GQ, 2 * P]), op0=ALU.mult, op1=ALU.add).then_inc(sc_free, 1)
                dve.drain()
                nc.vector.tensor_reduce(att[:, b, 0, :], sm[:, m, :, :], AX.X, ALU.max)
                dve.drain()
                nc.vector.tensor_tensor(att[:, b, 0, :], att[:, b, 0, :], sink, ALU.max)
                dve.drain()
                nc.vector.tensor_scalar(att[:, b, 1, :], att[:, b, 0, :], -1.0, None, ALU.mult)
                nc.vector.tensor_tensor(att[:, b, 2, :], sink, att[:, b, 0, :], ALU.subtract).then_inc(sm_ready, 1)

            def weighted(s):
                n, g = STEPS[s]
                b = s % 4
                dve.wait_ge(o_ready, s + 1)
                nc.vector.tensor_tensor(att[:, b, 3, :], att[:, b, 3, :], att[:, b, 4, :], ALU.add)
                dve.drain()
                nc.vector.reciprocal(att[:, b, 5, :], att[:, b, 3, :])
                dve.drain()
                nc.vector.tensor_tensor(
                    o_all[:, n, g * 256:(g + 1) * 256].rearrange("p (j d) -> p j d", j=GQ),
                    ps[:, out_bank(s), 0:256].rearrange("p (j d) -> p j d", j=GQ),
                    att[:, b, 5, :].unsqueeze(2).to_broadcast([P, GQ, HD]), ALU.mult).then_inc(o_done, 1)

            for s in range(NS + 2):
                if s < NS:
                    soft(s)
                if s >= 2:
                    weighted(s - 2)
                if s == CONV_STEP:
                    gate_values(LAST_C)
                    first_tap(LAST_C)
                elif s > CONV_STEP:
                    for k in range(1 + (s - CONV_STEP - 1) * CONV_TAPS, min(TAPS, 1 + (s - CONV_STEP) * CONV_TAPS)):
                        add_tap(LAST_C, k)
            dve.drain()
            dve.sem_inc(conv_dve, 1)

            def mixed_out(n):
                dve.wait_ge(ao_t, n + 1)
                nc.vector.tensor_tensor(
                    hnT[:, 0:4, n * P:(n + 1) * P], ps[:, 2 + n % 2, :].rearrange("p (m t) -> p m t", m=4),
                    par[:, G_ATT:G_ATT + 4].unsqueeze(2).to_broadcast([P, 4, P]), ALU.mult).then_inc(ao_mixed, 1)

            def add_attention(n):
                dve.wait_ge(x_in[n // HT], 16)
                dve.wait_ge(at_ready, n + 1)
                nc.vector.tensor_tensor(acc[:, n, :], acc[:, n, :], bank2(4 + 2 * (n % 2)), ALU.add).then_inc(at_added, 1)

            dve.wait_ge(ao_root, 1)
            nc.vector.reciprocal(small[:, 16:24], small[:, 8:16]).then_inc(ao_rec, 1)
            dve.wait_ge(ln_stat, 1)
            for c in range(CC):
                y = hnT[:, 4 + c, :]
                nc.vector.tensor_tensor(y, y, rb[:, :], ALU.subtract).then_inc(ln_y, 1)
            for n in range(NT):
                mixed_out(n)
            dve.wait_ge(ln_stat, 2)
            nc.vector.reciprocal(rb[:, :], rb[:, :])
            dve.drain()
            for c in range(CC):
                y = hnT[:, 4 + c, :]
                nc.vector.tensor_tensor(y, y, rb[:, :], ALU.mult).then_inc(ln_y, 1)
            for n in range(3):
                add_attention(n)
            dve.wait_ge(ln_stat, 3)
            nc.vector.reciprocal(rb[:, :], rb[:, :])
            dve.drain()
            for c in range(CC):
                y = hnT[:, 4 + c, :]
                nc.vector.scalar_tensor_tensor(out=y, in0=y, scalar=par[:, G_CONV + c:G_CONV + c + 1], in1=rb[:, :],
                                               op0=ALU.mult, op1=ALU.mult).then_inc(ln_y, 1)
            for n in range(3, NT):
                add_attention(n)

            def normed(n):
                dve.wait_ge(h_t, n + 1)
                nc.vector.tensor_tensor(
                    hnT[:, :, n * P:(n + 1) * P], bank2(4 + 2 * (n % 2)).rearrange("p (m t) -> p m t", m=DK),
                    par[:, G_FFN:G_FFN + DK].unsqueeze(2).to_broadcast([P, DK, P]), ALU.mult).then_inc(hnT_ready, 1)

            for n in range(NT):
                dve.wait_ge(wo_ready, n + 1)
                nc.vector.tensor_tensor(acc[:, n, :], acc[:, n, :], bank2(2 * (n % 2)), ALU.add).then_inc(h_ready, 1)
                if n:
                    normed(n - 1)
                dve.wait_ge(h_root, n + 1)
                nc.vector.reciprocal(small[:, 40 + n:41 + n], small[:, 32 + n:33 + n]).then_inc(h_rec, 1)
                if n in (HT + 2, HT + 3):
                    for k in range((n - HT - 2) * 4, (n - HT - 1) * 4):
                        dve.wait_ge(hnh_ready, k + 1)
                        nc.vector.tensor_tensor(hnl[:, k, :], hnT[:, k, 0:HALF], hnh[:, k, :].bitcast(F32),
                                                ALU.subtract).then_inc(hnl_ready, 1)
            normed(NT - 1)

            def scan(m, part):
                c, t0 = m % HP, m // HP * HT
                sv = ps[:, 2 + m % 2, :].rearrange("p (n k) -> p n k", n=HT)
                if part == 0:
                    dve.wait_ge(ks_ready, m + 1)
                    for n in range(HT):
                        nc.vector.max(s16[:, t0 + n, c, 0:8], sv[:, n, :])
                elif part == 1:
                    dve.drain()
                    for n in range(HT):
                        nc.vector.max_index(i16[:, n, c, 0:8], s16[:, t0 + n, c, 0:8], sv[:, n, :])
                    for n in range(HT):
                        last = nc.vector.match_replace(swork[:, n, :], s16[:, t0 + n, c, 0:8], sv[:, n, :], LOWEST)
                    last.then_inc(ks_free, 1)
                else:
                    dve.drain()
                    for n in range(HT):
                        nc.vector.max(s16[:, t0 + n, c, 8:16], swork[:, n, :])
                    dve.drain()
                    for n in range(HT):
                        nc.vector.max_index(i16[:, n, c, 8:16], s16[:, t0 + n, c, 8:16], swork[:, n, :])
                    if c == HP - 1:
                        dve.drain()
                        nc.vector.tensor_copy(i16p[:, t0:t0 + HT, :, :, :].rearrange("p n h k e -> p (n h k) e"),
                                              i16[:, :, :, :].rearrange("p n h k -> p (n h k)").unsqueeze(2)
                                              .to_broadcast([P, HT * HP * TOPK, 2]))

            def pick(i, step, h0=0, h1=PH, sums=None):
                if step == 0:
                    dve.drain()
                    for out, in0, in1 in candidate_sums(i, h0, h1):
                        nc.vector.tensor_tensor(out, in0, in1, ALU.add)
                elif step == 1:
                    if sums:
                        dve.wait_ge(sums_ready, sums)
                    dve.drain()
                    for h in range(h0, h1):
                        nc.vector.max(best[:, h, 0:8], cand[:, h, :])
                elif step == 2:
                    dve.drain()
                    for h in range(h0, h1):
                        nc.vector.max_index(bpos[:, h * TOPK:h * TOPK + 8], best[:, h, 0:8], cand[:, h, :])
                elif step == 3:
                    for h in range(h0, h1):
                        nc.vector.match_replace(cand2[:, h, :], best[:, h, 0:8], cand[:, h, :], LOWEST)
                elif step == 4:
                    dve.drain()
                    for h in range(h0, h1):
                        nc.vector.max(best[:, h, 8:16], cand2[:, h, :])
                elif step == 5:
                    dve.drain()
                    for h in range(h0, h1):
                        nc.vector.max_index(bpos[:, h * TOPK + 8:h * TOPK + 16], best[:, h, 8:16], cand2[:, h, :])
                    nc.vector.tensor_copy(den[:, 0, h0:h1], best[:, h0:h1, 0])
                elif step == 6:
                    dve.drain()
                    nc.vector.tensor_tensor(best[:, :, :], best[:, :, :],
                                            den[:, 0, :].unsqueeze(2).to_broadcast([P, PH, TOPK]),
                                            ALU.subtract).then_inc(best_ready, 1)
                    for k, (op, by) in enumerate(((ALU.logical_shift_right, 4), (ALU.logical_shift_right, 2),
                                                  (ALU.bitwise_and, WIDE - 1), (ALU.bitwise_and, TOPK - 1),
                                                  (ALU.logical_shift_right, 6))):
                        nc.vector.tensor_scalar(bdig[:, k, :], bpos[:, :], by, None, op)
                    dve.drain()
                    nc.vector.tensor_copy(bdigf, bdig[:, :, :])
                elif step == 7:
                    dve.drain()
                    nc.vector.scalar_tensor_tensor(out=ranks[:, 0, :], in0=bdigf[:, 1, :], scalar=-12.0, in1=bdigf[:, 0, :],
                                                   op0=ALU.add, op1=ALU.max)
                    nc.vector.scalar_tensor_tensor(out=ranks[:, 1, :], in0=bdigf[:, 4, :], scalar=-16.0, in1=bdigf[:, 3, :],
                                                   op0=ALU.mult, op1=ALU.add)
                    dve.drain()
                    nc.vector.tensor_tensor(ranks[:, 1, :], ranks[:, 1, :], bdigf[:, 2, :], ALU.max)
                elif step == 8:
                    dve.drain()
                    for d in range(2):
                        nc.vector.tensor_tensor(picks[:, d, :, :, :, :].rearrange("p h c a e -> p (h c) a e"),
                                                ranks[:, d, :].rearrange("p (c e) -> p c e", e=2).unsqueeze(2)
                                                .to_broadcast([P, P // 2, TOPK, 2]),
                                                iota2[:, 0:TOPK, :].unsqueeze(1).to_broadcast([P, P // 2, TOPK, 2]),
                                                ALU.is_equal)
                elif step == 9:
                    dve.drain()
                    it = i16p[:, bass.ds(i, 1), :, :, :].rearrange("p o (h s) k e -> p (o h) s (k e)", s=2)
                    for d in range(2):
                        chosen = picks[:, d, :, :, :, :].rearrange("p h c a e -> p h c (a e)")
                        nc.vector.tensor_tensor(chosen, chosen, it[:, :, d, :].unsqueeze(2)
                                                .to_broadcast([P, PH, TOPK // 2, 2 * TOPK]), ALU.mult)
                elif step == 10:
                    dve.wait_ge(exp_ready, i + 1)
                    nc.vector.tensor_reduce(den[:, 1, :], best[:, :, :], AX.X, ALU.add)
                    dve.drain()
                    nc.vector.reciprocal(den[:, 0, :], den[:, 1, :])
                elif step == 11:
                    dve.drain()
                    nc.vector.tensor_tensor(sel3[:, 2, :].rearrange("p (h k) -> p h k", h=PH), best[:, :, :],
                                            den[:, 0, :].unsqueeze(2).to_broadcast([P, PH, TOPK]), ALU.mult)
                elif step in (12, 13):
                    rows = picks[:, :, :, :, :, :].rearrange("p d h c a e -> p (d h c) (a e)")
                    for n in (TOPK, TOPK // 2) if step == 12 else (TOPK // 4, TOPK // 8):
                        dve.drain()
                        to = rows[:, :, 0:n] if n > 2 else sel3[:, 0:2, :].rearrange("p d (c e) -> p (d c) e", e=2)
                        last = nc.vector.tensor_tensor(to, rows[:, :, 0:n], rows[:, :, n:2 * n], ALU.add)
                    if step == 13:
                        last.then_inc(sel_ready, 1)

            def low_x(half, k):
                dve.wait_ge(xh_ready, half * DK + k + 1)
                nc.vector.tensor_tensor(xl[:, k, :], hnT[:, k, half * HALF:(half + 1) * HALF], xh[:, k, :].bitcast(F32),
                                        ALU.subtract).then_inc(xl_ready, 1)

            def low_u(half, g, c):
                n = half * NKEY + g * GC + c
                dve.wait_ge(uh_ready, n + 1)
                nc.vector.tensor_tensor(ul[:, c % 2, :, :].rearrange("p k e -> p (k e)"), u_raw[:, c % 2, :],
                                        uh[:, c % 2, :, :].rearrange("p k e -> p (k e)").bitcast(F32),
                                        ALU.subtract).then_inc(ul_ready, 1)

            def tile(i, u, ahead=2, mixed=False):
                dve.wait_ge(selT_ready, i + 1)
                for b in range(BLOCKS):
                    dve.wait_ge(hot_plain, i * BLOCKS + b + 1)
                    dve.wait_ge(hot_scaled, i * BLOCKS + b + 1)
                    nc.vector.tensor_tensor(
                        marks[:, b % RAW, :, :, :, :].rearrange("p d c k e -> p (d c) k e"),
                        selI[:, u, b, :, :].rearrange("p d (c e) -> p (d c) e", e=2).unsqueeze(2)
                        .to_broadcast([P, HOT, NKEY, 2]),
                        iota2[:, :, :].unsqueeze(1).to_broadcast([P, HOT, NKEY, 2]), ALU.is_equal).then_inc(hot_eq, 1)
                    if mixed:
                        n = i * BLOCKS + b
                        if ALONE + n // SPREAD - 2 < UNITS:
                            scan(ALONE + n // SPREAD - 2, n % SPREAD)
                    if ahead and b in LATE_STEPS:
                        pick(i + 1, LATE_STEPS[b])
                    if ahead > 1 and b >= BLOCKS - EARLY_STEPS:
                        step = b - (BLOCKS - EARLY_STEPS)
                        if mixed and i + 2 == HT:
                            pick(i + 2, step)
                        elif step:
                            pick(i + 2, step, sums=i + 1 if mixed and i + 2 < HT else i)
                    if ahead == 0:
                        if 6 <= b < 6 + DK:
                            low_x(0, b - 6)
                        elif b >= 6 + DK:
                            low_u(0, 0, b - 6 - DK)

            nc.vector.tensor_copy(iota2[:, :, :], iota.unsqueeze(2).to_broadcast([P, NKEY, 2]))
            for m in range(HP):
                for part in range(3):
                    scan(m, part)
                if m % 2:
                    for step in range(6):
                        pick(0, step, m // 2, m // 2 + 1)
            for step in range(6, 10):
                pick(0, step)
            for m in range(HP, ALONE - 2):
                for part in range(3):
                    scan(m, part)
            for step in range(10, STEPS_PICK):
                pick(0, step)
            for step in range(EARLY_STEPS):
                pick(1, step)
            for i in range(MIXED_TILES):
                tile(i, i % 2, mixed=True)
            with dve.Fori(MIXED_TILES // 2, NT // 2 - 1) as j:
                for u in range(2):
                    tile(j * 2 + u, u)
            tile(NT - 2, 0, ahead=1)
            tile(NT - 1, 1, ahead=0)

            def group(half, g, first=False, last=False):
                n0 = half * NKEY + g * GC
                for c in range(GC):
                    n = n0 + c
                    dve.wait_ge(vh_ready, n + 1)
                    nc.vector.tensor_tensor(vl[:, c, :], v_raw[:, c, :], vh[:, c, :].bitcast(F32),
                                            ALU.subtract).then_inc(vl_ready, 1)
                    if c == 0:
                        dve.wait_ge(g_in, 16 * (half * NG + g + 1))
                    dve.wait_ge(gelu_ready, n + 1)
                    nc.vector.tensor_tensor(hg[:, c % 2, :].rearrange("p (s t) -> p s t", t=SUB),
                                            hg[:, c % 2, :].rearrange("p (s t) -> p s t", t=SUB),
                                            gt[:, :, c, :], ALU.mult).then_inc(w_ready, 1)
                    dve.wait_ge(wh_ready, n + 1)
                    nc.vector.tensor_tensor(wl[:, c, :], hg[:, c % 2, :], wh[:, c, :].bitcast(F32),
                                            ALU.subtract).then_inc(wl_ready, 1)
                    if c < 2:
                        low_u(half, g, c + 2)
                    elif not last:
                        low_u(half, g + 1, c - 2)
                for k in range(8):
                    dve.wait_ge(op_ready, (half * NG + g) * 8 + k + 1)
                    dst = acc[:, half * HT + k % HT, (k // HT) * 512:(k // HT + 1) * 512]
                    nc.vector.tensor_tensor(dst, dst, ps[:, 2 + k % 4, :], ALU.add).then_inc(op_free, 1)
                    if last and half == 0:
                        low_x(1, k)

            def final_tiles(n0, n1, roots):
                dve.wait_ge(f_root, roots)
                nc.vector.reciprocal(small[:, 16 + n0:16 + n1], small[:, 8 + n0:8 + n1])
                dve.drain()
                for n in range(n0, n1):
                    nc.vector.scalar_tensor_tensor(out=acc[:, n, :], in0=acc[:, n, :], scalar=small[:, 16 + n:17 + n],
                                                   in1=fg[:, :], op0=ALU.mult, op1=ALU.mult).then_inc(f_ready, 1)

            for half in range(2):
                if half:
                    low_u(half, 0, 0)
                    low_u(half, 0, 1)
                if half == 0:
                    group(0, 0, first=True)
                with dve.Fori(1 - half, NG - 1) as g:
                    group(half, g)
                if half:
                    dve.wait_ge(fg_in, 16)
                    final_tiles(0, HT, 1)
                group(half, NG - 1, last=True)
            for n in range(HT, NT):
                final_tiles(n, n + 1, n - HT + 2)

        @block.tensor
        def _(pe):
            mm = nc.tensor.matmul
            pe.wait_ge(consts_in, 16)

            def sum_rows(bank, src, k, n):
                for hb in range(2):
                    last = mm(ps[:, bank + hb, :], ones, src[:, hb * 512:(hb + 1) * 512], start=k == 0, stop=k == n - 1)
                return last

            for k in range(DK):
                pe.wait_ge(sq_ready, k + 1)
                sum_rows(0, tmp[:, k % 2, :], k, DK).then_inc(sq_used, 1)

            def rotate(r):
                pe.wait_ge(raw_ready, r + 1)
                if r:
                    pe.wait_ge(rope_done, r)
                for hb in range(2):
                    last = mm(ps[:, 4 + hb, :], con[:, C_ROT:C_ROT + P], tmp[:, r % 2, hb * 512:(hb + 1) * 512],
                              start=True, stop=True)
                last.then_inc(rot_ready, 1)

            pe.wait_ge(rms_root, 1)
            for blk in range(NCH_ALONE):
                pe.wait_ge(w_in_slot[blk % 4], 16 * (blk // 4 + 1))
                back = blk - 2
                if 0 <= back < CH_K:
                    pe.wait_ge(gate_out, back + 1)
                elif back == CH_K:
                    pe.wait_ge(raw_ready, 1)
                elif back == CH_V:
                    pe.wait_ge(v_copied, 1)
                elif back >= CH_Q:
                    pe.wait_ge(raw_ready, back - CH_Q + 2)
                w = wbuf[:, blk % 4, :, :]
                if blk == CH_V:
                    for n in range(NT):
                        for k in range(DK):
                            last = mm(ps[:, 2 + n // 4, (n % 4) * P:(n % 4 + 1) * P], wide[:, k, n * P:(n + 1) * P],
                                      w[:, k, :], start=k == 0, stop=k == DK - 1)
                else:
                    for k in range(DK):
                        if blk == 0:
                            pe.wait_ge(hn_ready, k + 1)
                        for hb in range(2):
                            last = mm(ps[:, 2 * (blk % 2) + hb, :], w[:, k, :], wide[:, k, hb * 512:(hb + 1) * 512],
                                      start=k == 0, stop=k == DK - 1)
                last.then_inc(proj_ready, 1)
                if blk == CH_V:
                    rotate(0)
                if CH_Q < blk <= CH_Q + GQ:
                    rotate(blk - CH_Q)

            def scores(s):
                n, g = STEPS[s]
                if s >= 2:
                    pe.wait_ge(sc_free, s - 1)
                for j in range(GQ):
                    last = mm(ps[:, 2 * (s % 2) + j // 2, (j % 2) * 256:(j % 2 + 1) * 256],
                              qT[g * HD:(g + 1) * HD, j, n * P:(n + 1) * P], kT[g * HD:(g + 1) * HD, n * P:n * P + 2 * P],
                              start=True, stop=True)
                last.then_inc(sc_ready, 1)

            pe.wait_ge(gate_out, 6)
            pe.wait_ge(rope_done, 1 + GQ)
            pe.wait_ge(pads_ready, 1)

            def turn_probs(s):
                pe.wait_ge(p_ready, s + 1)
                if s:
                    pe.wait_ge(pt_copied, s)
                for j in range(2 * GQ):
                    last = nc.tensor.transpose(ps[:, 4 + j // 4, (j % 4) * P:(j % 4 + 1) * P],
                                               sm[:, s % 3, j // 2, (j % 2) * P:(j % 2 + 1) * P], ident)
                last.then_inc(pt_ready, 1)

            def weigh(s):
                n, g = STEPS[s]
                pe.wait_ge(pt_copied, s + 1)
                if s == PART_STEPS:
                    pe.wait_ge(part_out, 4)
                elif s > PART_STEPS:
                    pe.wait_ge(o_done, s - 1)
                elif s:
                    pe.wait_ge(o_done, s)
                for j in range(GQ):
                    for kb in range(2):
                        last = mm(ps[:, out_bank(s), j * HD:(j + 1) * HD], pT[:, 2 * j + kb, :],
                                  vv[:, n + kb, g * HD:(g + 1) * HD], start=kb == 0, stop=kb == 1)
                last.then_inc(o_ready, 1)

            def project_part(j, part):
                blk = NCH_ALONE + j // 2
                if part == 0:
                    pe.wait_ge(w_in_slot[blk % 4], 16 * (blk // 4 + 1))
                    if j:
                        pe.wait_ge(part_out, j)
                for k in range(part * DK // 2, (part + 1) * DK // 2):
                    last = mm(ps[:, 7, :], wbuf[:, blk % 4, k, :], wide[:, k, j % 2 * HALF:(j % 2 + 1) * HALF],
                              start=k == 0, stop=k == DK - 1)
                if part:
                    last.then_inc(part_ready, 1)

            scores(0)
            scores(1)
            for s in range(NS):
                turn_probs(s)
                if s + 2 < NS:
                    scores(s + 2)
                if s < 8:
                    project_part(s // 2, s % 2)
                weigh(s)

            pe.wait_ge(sc_free, NS)
            pe.wait_ge(conv_dve, CC - 2)
            pe.wait_ge(conv_pool, 2)
            for c in range(CC):
                last = sum_rows(0, hnT[:, 4 + c, :], c, CC)
            last.then_inc(ln_sum, 1)

            def turn_out(n):
                pe.wait_ge(ao_scaled, n + 1)
                if n >= 2:
                    pe.wait_ge(ao_mixed, n - 1)
                for m in range(4):
                    last = nc.tensor.transpose(ps[:, 2 + n % 2, m * P:(m + 1) * P], o_all[:, n, m * P:(m + 1) * P], ident)
                last.then_inc(ao_t, 1)

            def mix(n, bank, m0, ready):
                for hb in range(2):
                    for m in range(m0, m0 + 4):
                        last = mm(ps[:, bank + hb, :], hnT[:, m, n * P:(n + 1) * P],
                                  wide[:, m, hb * 512:(hb + 1) * 512], start=m == m0, stop=m == m0 + 3)
                last.then_inc(ready, 1)

            def attention_part(n):
                pe.wait_ge(ao_mixed, n + 1)
                if n >= 2:
                    pe.wait_ge(at_added, n - 1)
                mix(n, 4 + 2 * (n % 2), 0, at_ready)

            def sum_squares(r):
                for c in range(CC):
                    pe.wait_ge(ln_sq, r * CC + c + 1)
                    sum_rows(0, tmp[:, c % 2, :], c, CC).then_inc(ln_used, 1)

            for n in range(NT):
                turn_out(n)
            sum_squares(0)
            pe.wait_ge(wout_in, 16)
            for n in range(3):
                attention_part(n)
            sum_squares(1)
            for n in range(3, NT):
                attention_part(n)

            def turn(n):
                pe.wait_ge(h_scaled, n + 1)
                if n >= 2:
                    pe.wait_ge(hnT_ready, n - 1)
                else:
                    pe.wait_ge(at_added, NT)
                for m in range(DK):
                    last = nc.tensor.transpose(ps[:, 4 + 2 * (n % 2) + m // 4, (m % 4) * P:(m % 4 + 1) * P],
                                               tmp[:, n % 2, m * P:(m + 1) * P], ident)
                last.then_inc(h_t, 1)

            pe.wait_ge(ln_y, 3 * CC)
            for n in range(NT):
                if n >= 2:
                    pe.wait_ge(h_ready, n - 1)
                mix(n, 2 * (n % 2), 4, wo_ready)
                if n:
                    turn(n - 1)
            turn(NT - 1)

            def key_scores(m):
                pe.wait_ge(q_copied, m + 1)
                if m >= 2:
                    pe.wait_ge(ks_free, m - 1)
                for n in range(HT):
                    last = mm(ps[:, 2 + m % 2, n * P:(n + 1) * P], qc[:, m % 2, n * P:(n + 1) * P], keys[:, m % HP, :],
                              start=True, stop=True)
                last.then_inc(ks_ready, 1)

            def query(m, k0, k1):
                if k0 == 0:
                    pe.wait_ge(wq_in_slot[m % 4], 16 * (m // 4 + 1))
                    if m >= 2:
                        pe.wait_ge(q_copied, m - 1)
                t0 = m // HP * HALF
                for k in range(k0, k1):
                    last = mm(ps[:, m % 2, :], wqbuf[:, m % 4, k, :], hnT[:, k, t0:t0 + HALF], start=k == 0, stop=k == DK - 1)
                if k1 == DK:
                    last.then_inc(q_ready, 1)

            pe.wait_ge(hnT_ready, NT)
            pe.wait_ge(h_ready, NT)
            pe.wait_ge(keys_in, 16)

            def split_query(m):
                pe.wait_ge(wqh_ready, m + 1)
                if m >= 2:
                    pe.wait_ge(q_copied, m - 1)
                for k in range(DK):
                    if m == 0:
                        pe.wait_ge(hnl_ready, k + 1)
                    if k == 0:
                        pe.wait_ge(wql_ready, m + 1)
                    for w, xx in ((wqh, hnh), (wqh, hnl), (wql, hnh)):
                        last = mm(ps[:, m % 2, :], w[:, m % 2, k, :], xx[:, k, :], start=k == 0 and xx is hnh and w is wqh,
                                  stop=k == DK - 1 and w is wql)
                last.then_inc(q_ready, 1)

            for m in range(ALONE):
                if m < HP:
                    split_query(m)
                else:
                    query(m, 0, DK)
                if m:
                    key_scores(m - 1)

            pe.sem_inc(gp_ready, ROWS_CREDIT)

            def turn_selected(i):
                pe.wait_ge(sel_ready, i + 1)
                for d in range(3):
                    last = nc.tensor.transpose(ps[:, 5, d * P:(d + 1) * P], sel3[:, d, :], ident)
                last.then_inc(selT_ps, 1)

            def tile(i, u, ahead=2, mixed=False):
                for b in range(BLOCKS):
                    if mixed:
                        n = i * BLOCKS + b
                        unit, part = ALONE + n // SPREAD, n % SPREAD
                        if unit < UNITS:
                            query(unit, -(-DK * part // SPREAD), -(-DK * (part + 1) // SPREAD))
                        if part == 0 and unit <= UNITS:
                            key_scores(unit - 1)
                    pe.wait_ge(hot_plain, i * BLOCKS + b + 1 + RAW)
                    pe.wait_ge(hot_scaled, i * BLOCKS + b + 1 + RAW)
                    for e in range(HQ):
                        pe.wait_ge(gp_free, (i * BLOCKS + b) * HQ + e + 1)
                        for q in range(4):
                            last = mm(ps[:, 6 + e, q * P:(q + 1) * P], hot[:, b % ROWS, 1, e * 4 + q, :],
                                      hot[:, b % ROWS, 0, e * 4 + q, :], start=True, stop=True)
                        last.then_inc(gp_ready, 1)
                    if ahead and b == TURN_AFTER:
                        turn_selected(i + 1)

            turn_selected(0)
            for i in range(MIXED_TILES):
                tile(i, i % 2, mixed=True)
            with pe.Fori(MIXED_TILES // 2, NT // 2 - 1) as j:
                for u in range(2):
                    tile(j * 2 + u, u)
            tile(NT - 2, 0, ahead=1)
            tile(NT - 1, 1, ahead=0)

            def group(half, g, first=False):
                G = half * NG + g
                for c in range(GC):
                    n = half * NKEY + g * GC + c
                    pe.wait_ge(ul_ready, n + 1)
                    pe.wait_ge(uh_ready, n + 1)
                    if not first or c >= 2:
                        pe.wait_ge(gelu_ready, n - 1)
                    for k in range(DK):
                        for w, xx in ((uh, xh), (uh, xl), (ul, xh)):
                            last = mm(ps[:, c % 2, :], w[:, c % 2, k, :], xx[:, k, :],
                                      start=k == 0 and w is uh and xx is xh, stop=k == DK - 1 and w is ul)
                    last.then_inc(hp_ready, 1)

                def second(k, cs):
                    tt, dh = k % HT, k // HT
                    for c in cs:
                        for w, v in ((wh, vh), (wh, vl), (wl, vh)):
                            last = mm(ps[:, 2 + k % 4, :], w[:, c, tt * P:(tt + 1) * P], v[:, c, dh * 512:(dh + 1) * 512],
                                      start=c == 0 and w is wh and v is vh, stop=c == GC - 1 and w is wl)
                    return last

                pe.wait_ge(wl_ready, half * NKEY + g * GC + GC - 1)
                for k in range(2):
                    if not first:
                        pe.wait_ge(op_free, G * 8 + k - 3)
                    second(k, range(GC - 1))
                pe.wait_ge(wl_ready, half * NKEY + g * GC + GC)
                for k in range(2):
                    second(k, [GC - 1]).then_inc(op_ready, 1)
                for k in range(2, 8):
                    if not first or k >= 4:
                        pe.wait_ge(op_free, G * 8 + k - 3)
                    second(k, range(GC)).then_inc(op_ready, 1)

            for half in range(2):
                pe.wait_ge(xl_ready, (half + 1) * DK)
                if half == 0:
                    group(0, 0, first=True)
                with pe.Fori(1 - half, NG) as g:
                    group(half, g)


_INS = ["x", "norm_mix_g", "w_in", "conv_w", "conv_b", "conv_ln_g", "conv_ln_b", "attn_sinks", "attn_out_g",
        "conv_out_g", "w_out", "norm_ffn_g", "peer_w_q", "peer_sub_keys", "peer_u", "peer_v", "final_norm_g"]


def constants():
    import numpy as np

    con = np.zeros((P, C_END), np.float32)
    con[:, C_ID:C_ID + P] = np.eye(P)
    con[:, C_ONE:C_ONE + P] = 1
    con[:, C_IOTA:C_IOTA + P] = np.arange(P)
    half = HD // 2
    for m in range(P):
        first = m % HD < half
        con[m + half if first else m - half, C_ROT + m] = -1 if first else 1
    rel = np.arange(P)[:, None] + P - np.arange(2 * P)[None, :]
    band = (rel >= 0) & (rel < P)
    con[:, C_MASK:C_MASK + 2 * P] = np.where(band, 0, NEG)
    con[:, C_MASK0:C_MASK0 + 2 * P] = np.where(band & (np.arange(2 * P)[None, :] >= P), 0, NEG)
    inv = (10000.0 ** (-np.arange(half) / half)).astype(np.float32)
    ang = np.arange(T, dtype=np.float32)[None, :] * inv[:, None]
    con[:, C_COS:C_COS + T] = np.tile(np.cos(ang.astype(np.float64)), (P // half, 1))
    con[:, C_SIN:C_SIN + T] = np.tile(np.sin(ang.astype(np.float64)), (P // half, 1))
    return con


def kernel(**inputs):
    import numpy as np
    import concourse.bacc as bacc
    from concourse.bass_utils import run_bass_kernel_spmd

    a = {k: np.asarray(inputs[k]) for k in _INS}

    def rows(m):
        return m.reshape(m.shape[0] // P, P, -1).transpose(1, 0, 2)

    def cols(v):
        return v.reshape(-1, P).T

    x = a["x"].reshape(T, D)
    w_in = a["w_in"][0]
    q_cols = np.arange(HEADS * HD).reshape(KVH, GQ, HD).transpose(1, 0, 2).reshape(GQ, P)
    gated = [np.arange(g + c * P, g + (c + 1) * P) for c in range(CC) for g in (768, 1280)]
    blocks = gated[0:4] + [np.arange(512, 640), np.arange(640, 768), *q_cols] + gated[4:]
    w_blocks = np.stack([rows(w_in[:, b]) for b in blocks])
    w_q = np.stack([rows(b) for b in np.split(a["peer_w_q"][0], HP, axis=1)])
    keysT = a["peer_sub_keys"][0].reshape(HP, NKEY, P).transpose(2, 0, 1)
    uT = a["peer_u"][0].reshape(NKEY, P, DK, P).transpose(0, 3, 2, 1).reshape(NKEY, P, D)
    v_tab = a["peer_v"][0].reshape(NKEY, P, D)
    conv_w = a["conv_w"][0].T.reshape(CC, P, TAPS).transpose(1, 0, 2).reshape(P, CC * TAPS)
    params = np.concatenate(
        [cols(a["norm_mix_g"][0]), cols(a["norm_ffn_g"][0]), cols(a["attn_out_g"][0]), cols(a["conv_out_g"][0]),
         cols(a["conv_b"][0]), cols(a["conv_ln_g"][0]), cols(a["conv_ln_b"][0]),
         np.tile(a["attn_sinks"][0][None, :], (P, 1)), conv_w, np.full((P, 1), EPS, np.float32)], axis=1)
    data = {"x": x, "xT": rows(np.ascontiguousarray(x.T)), "w_in": w_blocks, "w_out": rows(a["w_out"][0]), "w_q": w_q,
            "keysT": keysT, "uT": uT, "v_tab": v_tab, "consts": constants(), "params": params,
            "final_g": a["final_norm_g"]}

    nc = bacc.Bacc("TRN2", target_bir_lowering=False, num_devices=1)
    arrays, args = {}, []
    for name, v in data.items():
        arrays[f"in_{name}"] = np.ascontiguousarray(v)
        args.append(nc.dram_tensor(f"in_{name}", v.shape, mybir.dt.from_np(v.dtype), kind="ExternalInput").ap())
    args.append(nc.dram_tensor("out_y", (T, D), F32, kind="ExternalOutput").ap())
    decoder_block(nc, *args)
    r = run_bass_kernel_spmd(nc, [arrays], core_ids=[0])
    return r.results[0]["out_y"].reshape(1, T, D)
```
